# Optimizing a Trainium2 kernel written in Bass

```python
import math
import jax, jax.numpy as jnp
from jax import lax
import numpy as np

D_MODEL = 1024
BATCH = 1
SEQ = 256
DEPTH = 1

CHUNK = 64
NORM_EPS = 1e-5
SB_HEADS = 8
SB_HEAD_DIM = 64
SB_WIDTH = SB_HEADS * SB_HEAD_DIM
Q_BLOCK = 128
POOL_WINDOWS = (2, 4, 8, 16)
POOL_GROUPS = len(POOL_WINDOWS)
POOL_GROUP_DIM = 128
POOL_WIDTH = POOL_GROUPS * POOL_GROUP_DIM
MIX_WIDTH = SB_WIDTH + POOL_WIDTH
IN_PROJ_WIDTH = 3 * SB_WIDTH + POOL_WIDTH
N_EXPERTS = 32
TOP_K = 4
D_FF = D_MODEL
SWIGLU_LIMIT = 7.0
SWIGLU_ALPHA = 1.702
EXPERT_BLOCK = 256

kernel_name = "stickbreak_pool_hybrid_moe"

def rms_norm(x, g):
    xf = x.astype(jnp.float32)
    y = xf * lax.rsqrt(jnp.mean(xf * xf, axis=-1, keepdims=True) + NORM_EPS)
    return (y * g.astype(jnp.float32)).astype(x.dtype)

def stick_breaking_attention(q, k, v):
    B, S, H, dh = q.shape
    scale = 1.0 / math.sqrt(dh)
    qh = q.transpose(0, 2, 1, 3).astype(jnp.float32)
    kh = k.transpose(0, 2, 1, 3).astype(jnp.float32)
    vh = v.transpose(0, 2, 1, 3).astype(jnp.float32)
    n_blocks = S // Q_BLOCK
    q_blocks = qh.reshape(B, H, n_blocks, Q_BLOCK, dh).transpose(2, 0, 1, 3, 4)
    starts = jnp.arange(n_blocks, dtype=jnp.int32) * Q_BLOCK
    key_pos = jnp.arange(S, dtype=jnp.int32)[None, :]

    def one_block(args):
        q_blk, t0 = args
        z = jnp.einsum('bhqd,bhkd->bhqk', q_blk, kh) * scale
        qry_pos = t0 + jnp.arange(Q_BLOCK, dtype=jnp.int32)[:, None]
        past = key_pos < qry_pos
        log_keep = jnp.where(past, jax.nn.log_sigmoid(-z), 0.0)
        after = lax.cumsum(log_keep, axis=3, reverse=True) - log_keep
        a = jnp.where(past, jnp.exp(jax.nn.log_sigmoid(z) + after), 0.0)
        return jnp.einsum('bhqk,bhkd->bhqd', a, vh)

    out = lax.map(one_block, (q_blocks, starts))
    out = out.transpose(1, 0, 3, 2, 4).reshape(B, S, H, dh)
    return out.astype(q.dtype)

def multiscale_pool(u, w_pool, pool_scale):
    B, S, _ = u.shape
    p = u.reshape(B, S, POOL_GROUPS, POOL_GROUP_DIM).astype(jnp.float32)
    c0 = jnp.concatenate([jnp.zeros((B, 1, POOL_GROUPS, POOL_GROUP_DIM), jnp.float32),
                          jnp.cumsum(p, axis=1)], axis=1)
    win = jnp.array(POOL_WINDOWS, dtype=jnp.int32)
    t = jnp.arange(S, dtype=jnp.int32)[:, None]
    lo = jnp.maximum(t + 1 - win[None, :], 0)
    cnt = (t + 1 - lo).astype(jnp.float32)
    lower = c0[:, lo, jnp.arange(POOL_GROUPS)[None, :], :]
    mix = (c0[:, 1:] - lower) / cnt[None, :, :, None] - p
    y = jnp.einsum('bsgc,gcd->bsgd', mix, w_pool.astype(jnp.float32))
    y = y * pool_scale.astype(jnp.float32)
    return y.reshape(B, S, POOL_WIDTH).astype(u.dtype)

def expert_ffn(xb, e, w_gate_up, b_gate_up, w_down, b_down):
    gu = xb @ w_gate_up[e] + b_gate_up[e]
    gate = jnp.minimum(gu[:, :D_FF], SWIGLU_LIMIT)
    up = jnp.clip(gu[:, D_FF:], -SWIGLU_LIMIT, SWIGLU_LIMIT)
    h = (up + 1.0) * gate * jax.nn.sigmoid(SWIGLU_ALPHA * gate)
    return h @ w_down[e] + b_down[e]

def moe_ffn(h, w_router, b_router, w_gate_up, b_gate_up, w_down, b_down):
    B, S, D = h.shape
    n_tok = B * S
    xf = h.reshape(n_tok, D)
    logits = (xf @ w_router + b_router).astype(jnp.float32)
    top_val, top_idx = lax.top_k(logits, TOP_K)
    gates = jax.nn.softmax(top_val, axis=-1)
    n_assign = n_tok * TOP_K
    flat_e = top_idx.reshape(-1).astype(jnp.int32)
    flat_tok = jnp.arange(n_assign, dtype=jnp.int32) // TOP_K
    order = jnp.argsort(flat_e)
    se, stok, sgate = flat_e[order], flat_tok[order], gates.reshape(-1)[order]
    counts = jnp.bincount(flat_e, length=N_EXPERTS)
    padded = (counts + EXPERT_BLOCK - 1) // EXPERT_BLOCK * EXPERT_BLOCK
    start = jnp.cumsum(counts) - counts
    pend = jnp.cumsum(padded)
    pstart = pend - padded
    dest = pstart[se] + (jnp.arange(n_assign, dtype=jnp.int32) - start[se])
    n_blocks = -(-n_assign // EXPERT_BLOCK) + N_EXPERTS
    buf = jnp.zeros((n_blocks * EXPERT_BLOCK, D), xf.dtype).at[dest].set(xf[stok])
    block_e = jnp.minimum(
        jnp.searchsorted(pend, jnp.arange(n_blocks, dtype=jnp.int32) * EXPERT_BLOCK, side='right'),
        N_EXPERTS - 1).astype(jnp.int32)
    yb = lax.map(lambda a: expert_ffn(a[0], a[1], w_gate_up, b_gate_up, w_down, b_down),
                 (buf.reshape(n_blocks, EXPERT_BLOCK, D), block_e))
    y_rows = yb.reshape(-1, D)[dest].astype(jnp.float32) * sgate[:, None]
    out = jax.ops.segment_sum(y_rows, stok, num_segments=n_tok)
    return out.reshape(B, S, D).astype(h.dtype)

def setup_inputs(seed: int = 0) -> dict:
    key = jax.random.key(seed)
    ks = jax.random.split(key, 17)
    f32 = jnp.float32
    nrm = lambda k, shape, s: jax.random.normal(k, shape, f32) * s
    L = DEPTH
    return {
        "x": jax.random.normal(ks[0], (BATCH, SEQ, D_MODEL), f32),
        "norm1_g": 1.0 + nrm(ks[1], (L, D_MODEL), 0.02),
        "w_in": nrm(ks[2], (L, D_MODEL, IN_PROJ_WIDTH), D_MODEL ** -0.5),
        "sb_norm_g": 1.0 + nrm(ks[3], (L, SB_WIDTH), 0.02),
        "w_pool": nrm(ks[4], (L, POOL_GROUPS, POOL_GROUP_DIM, POOL_GROUP_DIM), POOL_GROUP_DIM ** -0.5),
        "pool_scale": 1.0 + nrm(ks[5], (L, POOL_GROUPS, POOL_GROUP_DIM), 0.02),
        "w_out": nrm(ks[6], (L, MIX_WIDTH, D_MODEL), MIX_WIDTH ** -0.5),
        "norm2_g": 1.0 + nrm(ks[7], (L, D_MODEL), 0.02),
        "w_router": nrm(ks[8], (L, D_MODEL, N_EXPERTS), D_MODEL ** -0.5),
        "b_router": nrm(ks[9], (L, N_EXPERTS), 0.01),
        "w_gate_up": nrm(ks[10], (L, N_EXPERTS, D_MODEL, 2 * D_FF), D_MODEL ** -0.5),
        "b_gate_up": nrm(ks[11], (L, N_EXPERTS, 2 * D_FF), 0.02),
        "w_down": nrm(ks[12], (L, N_EXPERTS, D_FF, D_MODEL), D_FF ** -0.5),
        "b_down": nrm(ks[13], (L, N_EXPERTS, D_MODEL), 0.02),
        "final_norm_g": 1.0 + nrm(ks[14], (D_MODEL,), 0.02),
    }

def reference(x, norm1_g, w_in, sb_norm_g, w_pool, pool_scale, w_out, norm2_g,
              w_router, b_router, w_gate_up, b_gate_up, w_down, b_down, final_norm_g):
    B, S, _ = x.shape
    for layer in range(DEPTH):
        h = rms_norm(x, norm1_g[layer])
        proj = h @ w_in[layer]
        q = proj[..., :SB_WIDTH].reshape(B, S, SB_HEADS, SB_HEAD_DIM)
        k = proj[..., SB_WIDTH:2 * SB_WIDTH].reshape(B, S, SB_HEADS, SB_HEAD_DIM)
        v = proj[..., 2 * SB_WIDTH:3 * SB_WIDTH].reshape(B, S, SB_HEADS, SB_HEAD_DIM)
        u = proj[..., 3 * SB_WIDTH:]
        sb = stick_breaking_attention(q, k, v)
        sb = rms_norm(sb, sb_norm_g[layer].reshape(SB_HEADS, SB_HEAD_DIM)).reshape(B, S, SB_WIDTH)
        pool = multiscale_pool(u, w_pool[layer], pool_scale[layer])
        x = x + jnp.concatenate([sb, pool], axis=-1) @ w_out[layer]
        h2 = rms_norm(x, norm2_g[layer])
        x = x + moe_ffn(h2, w_router[layer], b_router[layer], w_gate_up[layer],
                        b_gate_up[layer], w_down[layer], b_down[layer])
    return rms_norm(x, final_norm_g)


_drawn_inputs = setup_inputs


def setup_inputs(seed=0):
    import zlib

    import numpy as np

    out = dict(_drawn_inputs(seed))
    spreads = {}
    factors = {'b_router': 2.869, 'b_gate_up': 6.653, 'b_down': 7.547, 'final_norm_g': 2.869}
    for name, (base, spread) in spreads.items():
        noise = np.random.default_rng([zlib.crc32(name.encode()), seed]).standard_normal(out[name].shape)
        drawn = base * np.exp(spread * noise) if base else spread * noise
        out[name] = __import__('jax').numpy.asarray(drawn.astype(out[name].dtype))
    for name, factor in factors.items():
        out[name] = (out[name] * factor).astype(out[name].dtype)
    return out
```

```python
from contextlib import ExitStack

import concourse.bass as bass
from concourse import mybir

F32 = mybir.dt.float32
I32 = mybir.dt.int32
ALU = mybir.AluOpType
ACT = mybir.ActivationFunctionType
AX_X = mybir.AxisListType.X

P = 128
EPS = 1e-5
TOP_K = 4
WINDOWS = (2, 4, 8, 16)
LIMIT = 7.0
ALPHA = 1.702
SLOTS = 64
SENTINEL = 2.0e38
TAKEN = 3.0e38


def build(nc, x, norm1_g, w_in, sb_norm_g, w_pool, pool_scale, w_out, norm2_g, w_router, b_router,
          w_gate_up, b_gate_up, w_down, b_down, final_norm_g, out):
    _, S, D = x.shape
    NIN = w_in.shape[2]
    _, NE, _, F2 = w_gate_up.shape
    F = F2 // 2
    SBW = sb_norm_g.shape[1]
    _, NG, GC, _ = w_pool.shape
    HD = 64
    TT = S // P
    KD = D // P
    KF = F // P
    NPAIR = SBW // P
    HALF = 512
    assert (S, D, F, NIN, NE, SBW, NG, GC) == (256, 1024, 1024, 2048, 32, 512, 4, 128)

    CHUNK = 2048
    RING = 16
    UP_CHUNKS = KD
    DOWN_CHUNKS = KF // 2
    PER_EXPERT = UP_CHUNKS + DOWN_CHUNKS
    BODY = 4
    NBODY = NE // BODY
    PER_BODY = BODY * PER_EXPERT
    GEN = PER_BODY // RING
    FIRST_SLOT = RING - 4
    assert PER_BODY % RING == 0 and UP_CHUNKS == 8 and DOWN_CHUNKS == 4

    def slot_of(n):
        return (FIRST_SLOT + n) % RING

    rows = {
        "wgu": w_gate_up.rearrange("l e d f -> (l e d) f"),
        "wd": w_down.rearrange("l e f d -> (l e f) d"),
        "bgu": b_gate_up.rearrange("l e (r c) -> (l e r) c", c=HALF),
    }

    with ExitStack() as ctx:
        def sb(name, shape, dt=F32):
            return ctx.enter_context(nc.sbuf_tensor(name, shape, dt))

        def sem(name):
            return ctx.enter_context(nc.semaphore(name))

        ring = sb("ring", [P, RING * CHUNK])
        xres = sb("xres", [P, TT, D])
        xn = sb("xn", [P, TT, D])
        area = sb("area", [P, 10240])

        def part(lo, n, a=None):
            v = area[:, lo:lo + n]
            return v if a is None else v.rearrange("p (a b) -> p a b", a=a)

        hT = part(0, KD * S, KD)
        mixT = hT
        qkT = part(2048, 2048, 8)
        vtok = part(4096, TT * SBW, TT)
        uT = part(5120, NG * (S + 16), NG)
        lw = [part(6208 + 768 * i, 768, 2) for i in range(2)]
        aw = [part(7744 + 768 * i, 768, 2) for i in range(2)]
        win = [part(9280 + 272 * i, 272) for i in range(2)]
        sq = part(9824, S)
        h2T = part(0, KD * S, KD)
        xT = [part(2048 + 1024 * i, 1024, KD) for i in range(2)]
        gatec, upc, sig, act_t, act_h = [part(4096 + HALF * i, HALF) for i in range(5)]
        hidT = part(6656, HALF, 4)
        ypair = part(7168, D)
        scat = [part(8192 + S * i, S) for i in range(2)]
        pick = [part(8704 + 2 * P * i, 2 * P, TT) for i in range(2)]
        hidT_all = part(2048, 1024, KF)

        wide = sb("wide", [P, D])
        wpool = sb("wpool", [P, NG, GC])
        wrouter = sb("wrouter", [P, KD, NE])
        brow = sb("brow", [1, NE])
        bias = sb("bias", [4, 2, HALF])
        bsel = sb("bsel", [4, 6, P])
        vecs = sb("vecs", [24, P])
        vecT = sb("vecT", [P, 24])
        ident = sb("ident", [P, P])
        negtri = sb("negtri", [P, P])
        negones = sb("negones", [P, P])
        ones = sb("ones", [P, P])
        before = sb("before", [P, P])
        headmean = sb("headmean", [P, P])
        iota_i = sb("iota_i", [P, S], I32)
        iota = sb("iota", [P, S])
        edge = sb("edge", [P, NG, 16])
        lg = sb("lg", [P, TT, NE + 4])
        lgr = sb("lgr", [P, TT, NE + 4])
        top8 = sb("top8", [P, TT, 8])
        negtop = sb("negtop", [P, TT])
        mask = sb("mask", [P, TT, NE])
        ex = sb("ex", [P, TT, NE])
        exm = sb("exm", [P, TT, NE])
        gate = sb("gate", [P, TT, NE])
        gateT = sb("gateT", [NE, S])
        rank = sb("rank", [P, TT, NE + 2])
        gtab = sb("gtab", [P, TT, NE // 2 + 1, 3])
        info = sb("info", [P, 3])
        stat = sb("stat", [P, 16])
        epsc = sb("epsc", [P, 1])
        most = sb("most", [1, 2])
        flag = sb("flag", [1, 1], I32)
        bank = [ctx.enter_context(nc.psum_tensor(f"bank{i}", [P, HALF], F32)) for i in range(8)]
        G1, G2, SBG, PSC = vecT[:, 0:8], vecT[:, 8:16], vecT[:, 16:20], vecT[:, 20:24]
        BG, BU, BY, BM = bank[4], bank[5], bank[6], bank[7]

        x_in = [sem(f"x_in{i}") for i in range(TT)]
        vecs_in = [sem(f"vecs_in{i}") for i in range(4)]
        wpool_in, wrouter_in, brow_in, bdown_in, fg_in = map(
            sem, ("wpool_in", "wrouter_in", "brow_in", "bdown_in", "fg_in"))
        win_in = [sem(f"win_in{i}") for i in range(8)]
        wout_in = [sem(f"wout_in{i}") for i in range(4)]
        chunk_in = [sem(f"chunk_in{i}") for i in range(RING)]
        bias_in = [sem(f"bias_in{i}") for i in range(2)]
        chunks_used = sem("chunks_used")
        bias_used = sem("bias_used")
        out_done = sem("out_done")

        consts, pool_c, iota_f, edge_c = map(sem, ("consts", "pool_c", "iota_f", "edge_c"))
        vec_t, vec_c = sem("vec_t"), sem("vec_c")
        ssq, rtd, rinv, xn_ok = map(sem, ("ssq", "rtd", "rinv", "xn_ok"))
        tr, tr_c = sem("tr"), sem("tr_c")
        proj = sem("proj")
        q_c, k_c, v_c, v2_c, u_c = map(sem, ("q_c", "k_c", "v_c", "v2_c", "u_c"))
        win_add, win_out, mix_ok = map(sem, ("win_add", "win_out", "mix_ok"))
        z_ok, t1, t2, t3, l_add, l_ok, zc_ok, a_exp, a_ok, o_ok, o_c, sq_ok, ms_ok = map(
            sem, ("z_ok", "t1", "t2", "t3", "l_add", "l_ok", "zc_ok", "a_exp", "a_ok", "o_ok", "o_c",
                  "sq_ok", "ms_ok"))
        hs_rt, hs_inv, sbn = map(sem, ("hs_rt", "hs_inv", "sbn"))
        pool_ok, poolT_ok = sem("pool_ok"), sem("poolT_ok")
        wo_ok, x2_ok = sem("wo_ok"), sem("x2_ok")
        lg_ok, lg_c, mx, ntop, t8, mr, mask_ok, ex_ok, exm_ok, den, gate_ok = map(
            sem, ("lg_ok", "lg_c", "mx", "ntop", "t8", "mr", "mask_ok", "ex_ok", "exm_ok", "den",
                  "gate_ok"))
        rank_ok, rank_p, rank_c, cnt_m, flag_ok, gtab_ok, gT_ok, gT_c, bd_ok = map(
            sem, ("rank_ok", "rank_p", "rank_c", "cnt_m", "flag_ok", "gtab_ok", "gT_ok", "gT_c",
                  "bd_ok"))
        pick_ok, info_ok, info_c, scat_ok, ga_ok, gb_ok, xa_ok, xb_ok = map(
            sem, ("pick_ok", "info_ok", "info_c", "scat_ok", "ga_ok", "gb_ok", "xa_ok", "xb_ok"))
        gc_ok, uc_ok, sig_ok, t_ok, h_ok, hT_ok, hT_c, y_lo, y_hi, comb_ok = map(
            sem, ("gc_ok", "uc_ok", "sig_ok", "t_ok", "h_ok", "hT_ok", "hT_c",
                  "y_lo", "y_hi", "comb_ok"))
        n_acc0, n_up, n_gc, n_uc, n_sig, n_t, n_h, n_hT, n_hTc, n_y, n_acc = map(
            sem, ("n_acc0", "n_up", "n_gc", "n_uc", "n_sig", "n_t", "n_h", "n_hT", "n_hTc", "n_y",
                  "n_acc"))
        sum_ok, fsq, frt, finv, fin = map(sem, ("sum_ok", "fsq", "frt", "finv", "fin"))

        def up_w(n, gu, half):
            lo = slot_of(n) * CHUNK + gu * F + half * HALF
            return ring[:, lo:lo + HALF]

        def down_w(n, s, half):
            lo = slot_of(n) * CHUNK + s * D + half * HALF
            return ring[:, lo:lo + HALF]

        block = ctx.enter_context(nc.Block())

        @block.sync
        def _(sp):
            for tt in range(TT):
                sp.dma_start(xres[:, tt, :], x[0, tt * P:(tt + 1) * P, :]).then_inc(x_in[tt], 16)
            for k in range(KD):
                sp.dma_start(ring[:, k * CHUNK:(k + 1) * CHUNK],
                             w_in[0, k * P:(k + 1) * P, :]).then_inc(win_in[k], 16)
            for c in (2, 3, 0, 1):
                sp.dma_start(
                    ring[:, (8 + c) * CHUNK:(9 + c) * CHUNK].rearrange("p (s n) -> p s n", s=2),
                    w_out[0, c * 2 * P:(c + 1) * 2 * P, :].rearrange("(s p) n -> p s n", s=2)
                ).then_inc(wout_in[c], 16)

            def load_expert(e, m0, first):
                r = m0 // PER_EXPERT
                if not first or r >= 2:
                    sp.wait_ge(bias_used, e - 1)
                sp.dma_start(bias[:, r % 2, :], rows["bgu"][bass.ds(e * 4, 4), :]).then_inc(
                    bias_in[r % 2], 16)
                for c in range(PER_EXPERT):
                    m = m0 + c
                    s = slot_of(m)
                    n = e * PER_EXPERT + c
                    if first and m < RING:
                        if m >= 4:
                            sp.wait_ge(proj if m < 12 else wo_ok, 1)
                    else:
                        sp.wait_ge(chunks_used, n - (RING - 1))
                    dst = ring[:, s * CHUNK:(s + 1) * CHUNK]
                    if c < UP_CHUNKS:
                        src = rows["wgu"][bass.ds(e * D + c * P, P), :]
                    else:
                        src = rows["wd"][bass.ds(e * F + (c - UP_CHUNKS) * 2 * P, 2 * P), :].rearrange(
                            "(s p) n -> p s n", s=2)
                        dst = dst.rearrange("p (s n) -> p s n", s=2)
                    sp.dma_start(dst, src).then_inc(chunk_in[s], 16)

            for r in range(BODY):
                load_expert(r, r * PER_EXPERT, True)
            with sp.Fori(1, NBODY) as i:
                for r in range(BODY):
                    load_expert(i * BODY + r, r * PER_EXPERT, False)
            sp.wait_ge(fin, 1)
            sp.dma_start(out[0, 0:P, :], xn[:, 0, :]).then_inc(out_done, 16)
            sp.wait_ge(fin, 2)
            sp.dma_start(out[0, P:2 * P, :], xn[:, 1, :]).then_inc(out_done, 16)
            sp.wait_ge(out_done, 32)

        @block.gpsimd
        def _(pool):
            g = nc.gpsimd
            g.memset(ident[:], 0.0).then_inc(pool_c, 1)
            g.memset(negtri[:], -1.0).then_inc(pool_c, 1)
            g.memset(before[:], 1.0).then_inc(pool_c, 1)
            g.memset(bsel[:], 0.0).then_inc(pool_c, 1)
            pool.wait_ge(pool_c, 4)
            g.affine_select(ident[:], ident[:], compare_op=ALU.not_equal, fill=1.0, base=0,
                            pattern=[[-1, P]], channel_multiplier=1).then_inc(consts, 1)
            g.affine_select(negtri[:], negtri[:], compare_op=ALU.is_ge, fill=0.0, base=0,
                            pattern=[[-1, P]], channel_multiplier=1).then_inc(consts, 1)
            g.affine_select(before[:], before[:], compare_op=ALU.is_gt, fill=0.0, base=0,
                            pattern=[[1, P]], channel_multiplier=-1).then_inc(consts, 1)
            g.affine_select(bsel[:, 0:2, 0:SLOTS], bsel[:, 0:2, 0:SLOTS], compare_op=ALU.not_equal,
                            fill=1.0, base=0, pattern=[[-2, 2], [0, SLOTS]],
                            channel_multiplier=1).then_inc(consts, 1)
            g.affine_select(bsel[:, 0:2, SLOTS:P], bsel[:, 0:2, SLOTS:P], compare_op=ALU.not_equal,
                            fill=1.0, base=-1, pattern=[[-2, 2], [0, SLOTS]],
                            channel_multiplier=1).then_inc(consts, 1)
            g.affine_select(bsel[:, 2:6, :], bsel[:, 2:6, :], compare_op=ALU.not_equal,
                            fill=1.0, base=0, pattern=[[-1, 4], [0, P]],
                            channel_multiplier=1).then_inc(consts, 1)
            g.iota(iota_i[:], pattern=[[1, S]], base=0, channel_multiplier=0).then_inc(pool_c, 1)
            for tt in range(TT):
                g.iota(gtab[:, tt, :, 2], pattern=[[0, NE // 2 + 1]], base=tt * P,
                       channel_multiplier=1,
                       allow_small_or_imprecise_dtypes=True).then_inc(pool_c, 1)
            pool.wait_ge(pool_c, 5)
            g.tensor_copy(iota[:], iota_i[:]).then_inc(iota_f, 1)
            for b in range(2):
                g.memset(win[b][:, 0:16], 0.0).then_inc(pool_c, 1)
            g.memset(uT[:, :, 0:16], 0.0).then_inc(pool_c, 1)
            pool.wait_ge(pool_c, 10)
            n = 0
            for gr in range(NG):
                pool.wait_ge(u_c, 1)
                src = uT[:, gr, :]
                for lev in range(gr + 1):
                    w = 1 << lev
                    if n >= 1:
                        pool.wait_ge(win_add, n)
                    if lev == 0 and gr >= 1:
                        pool.wait_ge(mix_ok, gr)
                    dst = win[lev % 2]
                    g.tensor_tensor(dst[:, 16:16 + S], src[:, 16:16 + S], src[:, 16 - w:16 - w + S],
                                    ALU.add).then_inc(win_add, 1)
                    n += 1
                    src = dst

        @block.scalar
        def _(act):
            a = nc.scalar
            for i, (src, lo, n) in enumerate(((norm1_g, 0, 8), (norm2_g, 8, 8), (sb_norm_g, 16, 4),
                                              (pool_scale, 20, 4))):
                v = src[0, :, :] if len(src.shape) == 3 else src.rearrange("l (r c) -> (l r) c", c=P)
                act.dma_start(vecs[lo:lo + n, :], v).then_inc(vecs_in[i], 16)
            act.dma_start(wpool[:], w_pool[0].rearrange("g c d -> c g d")).then_inc(wpool_in, 16)
            act.dma_start(wrouter[:], w_router[0].rearrange("(k p) e -> p k e", p=P)).then_inc(
                wrouter_in, 16)
            act.dma_start(brow[:], b_router).then_inc(brow_in, 16)
            act.dma_start(wide[0:NE, :], b_down[0]).then_inc(bdown_in, 16)

            def sums_of_squares(src, first, scratch, done):
                for tt in range(TT):
                    a.activation(scratch[:, tt, :], src[:, tt, :], ACT.Square,
                                 accum_out=stat[:, first + tt:first + tt + 1]).then_inc(done, 1)

            for tt in range(TT):
                act.wait_ge(x_in[tt], 16)
                a.activation(xn[:, tt, :], xres[:, tt, :], ACT.Square,
                             accum_out=stat[:, tt:tt + 1]).then_inc(ssq, 1)
            act.wait_ge(ssq, 2)
            act.wait_ge(edge_c, 3)
            a.activation(stat[:, 2:4], stat[:, 0:2], ACT.Sqrt, scale=1.0 / D,
                         bias=epsc[:]).then_inc(rtd, 1)

            act.wait_ge(proj, 1)
            for b in range(2):
                a.activation(qkT[:, 2 * b:2 * b + 2, :],
                             bank[b][:].rearrange("p (a t) -> p a t", a=2), ACT.Copy,
                             scale=float(HD) ** -0.5).then_inc(q_c, 1)
            a.activation(vtok[:, 0, :], bank[6][:], ACT.Copy).then_inc(v_c, 1)

            def softplus_tail(j):
                t = lw[j % 2]
                act.wait_ge(z_ok, j + 1)
                if j >= 2:
                    act.wait_ge(zc_ok, j - 1)
                for h in range(2):
                    a.activation(t[:, h, :], bank[2 * (j % 2) + h][:, 0:384], ACT.Abs).then_inc(t1, 1)
                act.wait_ge(t1, 2 * j + 2)
                a.activation(t[:], t[:], ACT.Exp, scale=-1.0).then_inc(t2, 1)
                act.wait_ge(t2, j + 1)
                a.activation(t[:], t[:], ACT.Ln, bias=1.0).then_inc(t3, 1)

            def weights_exp(j):
                act.wait_ge(zc_ok, j + 1)
                if j >= 2:
                    act.wait_ge(o_ok, j - 1)
                for h in range(2):
                    a.activation(aw[j % 2][:, h, :], bank[2 * (j % 2) + h][:, 0:384],
                                 ACT.Exp).then_inc(a_exp, 1)

            def square_out(j):
                act.wait_ge(o_c, j + 1)
                if j >= 1:
                    act.wait_ge(ms_ok, j)
                a.activation(sq[:], mixT[:, j, :], ACT.Square).then_inc(sq_ok, 1)

            softplus_tail(0)
            for j in range(NPAIR):
                if j + 1 < NPAIR:
                    softplus_tail(j + 1)
                weights_exp(j)
                if j >= 1:
                    square_out(j - 1)
            square_out(NPAIR - 1)
            act.wait_ge(ms_ok, NPAIR)
            for b in range(2):
                a.activation(lw[b][:].rearrange("p a b -> p (a b)")[:, 0:HALF], bank[6 + b][:],
                             ACT.Sqrt, bias=epsc[:]).then_inc(hs_rt, 1)
            act.wait_ge(x2_ok, 2 * TT)
            for tt in range(TT):
                a.activation(xn[:, tt, :], xres[:, tt, :], ACT.Square,
                             accum_out=stat[:, 4 + tt:5 + tt]).then_inc(ssq, 1)
            act.wait_ge(ssq, 4)
            a.activation(stat[:, 6:8], stat[:, 4:6], ACT.Sqrt, scale=1.0 / D,
                         bias=epsc[:]).then_inc(rtd, 1)
            act.wait_ge(ntop, 1)
            for tt in range(TT):
                a.activation(ex[:, tt, :], lg[:, tt, 0:NE], ACT.Exp,
                             bias=negtop[:, tt:tt + 1]).then_inc(ex_ok, 1)

            act.wait_ge(bd_ok, 1)
            act.dma_start(wide[:], final_norm_g.rearrange("(a d) -> a d", a=1).broadcast_to([P, D])
                          ).then_inc(fg_in, 16)

            act.wait_ge(flag_ok, 1)
            crowded = act.value_load(flag[0:1, 0:1], min_val=0, max_val=1)

            def fast_expert(e, r):
                act.wait_ge(gc_ok, e + 1)
                a.activation(sig, gatec, ACT.Sigmoid, scale=ALPHA).then_inc(sig_ok, 1)
                act.wait_ge(hT_ok, e + 1)
                a.activation(hidT, BG[:].rearrange("p (j t) -> p j t", j=4), ACT.Copy).then_inc(hT_c, 1)
                act.wait_ge(chunks_used, (e + 1) * PER_EXPERT)
                lo = (r % 2) * SLOTS
                a.activation(ypair[lo:lo + SLOTS, 0:HALF], BY[0:SLOTS, :], ACT.Copy).then_inc(y_lo, 1)

            with act.If(crowded):
                with act.Fori(0, NE) as e:
                    for tt in range(TT):
                        for hf in range(2):
                            n = e * 4 + (2 * tt + hf + 1)
                            act.wait_ge(n_gc, n)
                            a.activation(sig, gatec, ACT.Sigmoid, scale=ALPHA).then_inc(n_sig, 1)
                            act.wait_ge(n_hT, n)
                            a.activation(hidT_all[:, 4 * hf:4 * hf + 4, :],
                                         BG[:].rearrange("p (j t) -> p j t", j=4),
                                         ACT.Copy).then_inc(n_hTc, 1)
            with act.Else():
                with act.Fori(0, NE // 2) as q:
                    for r in range(2):
                        fast_expert(q * 2 + r, r)

            act.wait_ge(sum_ok, 2 * TT)
            for tt in range(TT):
                a.activation(xn[:, tt, :], xres[:, tt, :], ACT.Square,
                             accum_out=stat[:, 8 + tt:9 + tt]).then_inc(fsq, 1)
                act.wait_ge(fsq, tt + 1)
                a.activation(stat[:, 10 + tt:11 + tt], stat[:, 8 + tt:9 + tt], ACT.Sqrt,
                             scale=1.0 / D, bias=epsc[:]).then_inc(frt, 1)

        @block.vector
        def _(dve):
            v = nc.vector
            v.memset(ones[:], 1.0).then_inc(consts, 1)
            v.memset(headmean[:], 0.0).then_inc(edge_c, 1)
            dve.wait_ge(edge_c, 1)
            for h in range(2):
                v.memset(headmean[h * HD:(h + 1) * HD, h * HD:(h + 1) * HD],
                         1.0 / HD).then_inc(consts, 1)
            v.memset(negones[:], -1.0).then_inc(edge_c, 1)
            v.memset(epsc[:], EPS).then_inc(edge_c, 1)
            v.memset(rank[:], -1.0).then_inc(edge_c, 1)
            v.memset(lg[:, :, NE:NE + 4], SENTINEL).then_inc(edge_c, 1)
            dve.wait_ge(iota_f, 1)
            for g in range(NG):
                v.tensor_scalar(edge[:, g, :], iota[:, 0:16], 1.0, float(WINDOWS[g]), ALU.add,
                                ALU.min).then_inc(edge_c, 1)
            dve.wait_ge(edge_c, 9)
            v.reciprocal(edge[:], edge[:]).then_inc(edge_c, 1)
            dve.wait_ge(edge_c, 10)
            for g in range(NG):
                v.tensor_scalar(edge[:, g, :], edge[:, g, :], float(WINDOWS[g]), None,
                                ALU.mult).then_inc(edge_c, 1)
            v.memset(gtab[:, :, :, 0:2], 0.0).then_inc(edge_c, 1)
            dve.wait_ge(vec_t, 1)
            v.tensor_copy(vecT[:], bank[7][:, 0:24]).then_inc(vec_c, 1)

            def normalise(root, first, done):
                dve.wait_ge(rtd, root)
                v.reciprocal(stat[:, first:first + 2], stat[:, first:first + 2]).then_inc(rinv, 1)
                dve.wait_ge(rinv, root)
                for tt in range(TT):
                    v.tensor_scalar(xn[:, tt, :], xres[:, tt, :], stat[:, first + tt:first + tt + 1],
                                    None, ALU.mult).then_inc(xn_ok, 1)

            def gained(base, dst, gains):
                for n in range(4):
                    tt, kh = n // 2, n % 2
                    dve.wait_ge(tr, base + n + 1)
                    v.tensor_tensor(
                        dst[:, 4 * kh:4 * kh + 4, tt * P:(tt + 1) * P],
                        bank[(0, 4)[base > 0] + n][:].rearrange("p (k t) -> p k t", k=4),
                        gains[:, 4 * kh:4 * kh + 4].unsqueeze(2).to_broadcast([P, 4, P]),
                        ALU.mult).then_inc(tr_c, 1)

            normalise(1, 2, 2)
            dve.wait_ge(vec_c, 1)
            gained(0, hT, G1)

            dve.wait_ge(proj, 1)
            for b in range(2):
                v.tensor_copy(qkT[:, 4 + 2 * b:6 + 2 * b, :],
                              bank[2 + b][:].rearrange("p (a t) -> p a t", a=2)).then_inc(k_c, 1)
            v.tensor_copy(vtok[:, 1, :], bank[7][:]).then_inc(v2_c, 1)
            for b in range(2):
                u = v.tensor_copy(uT[:, 2 * b:2 * b + 2, 16:16 + S],
                                  bank[4 + b][:].rearrange("p (a t) -> p a t", a=2))
            u.then_inc(u_c, 1)

            def softplus_head(j):
                t = lw[j % 2]
                dve.wait_ge(t3, j + 1)
                for h in range(2):
                    v.scalar_tensor_tensor(out=t[:, h, :], in0=bank[2 * (j % 2) + h][:, 0:384],
                                           scalar=0.0, in1=t[:, h, :], op0=ALU.max,
                                           op1=ALU.add).then_inc(l_add, 1)
                dve.wait_ge(l_add, 2 * j + 2)
                for c in (0, 256):
                    v.tensor_tensor(t[:, :, c:c + P], t[:, :, c:c + P],
                                    before[:].unsqueeze(1).to_broadcast([P, 2, P]),
                                    ALU.mult).then_inc(l_ok, 1)

            def weights_mask(j):
                t = aw[j % 2]
                dve.wait_ge(a_exp, 2 * j + 2)
                for c in (0, 256):
                    for h in range(2):
                        v.scalar_tensor_tensor(out=t[:, h, c:c + P], in0=t[:, h, c:c + P], scalar=1.0,
                                               in1=before[:], op0=ALU.min,
                                               op1=ALU.mult).then_inc(a_ok, 1)

            def heads_out(j):
                dve.wait_ge(o_ok, j + 1)
                v.tensor_copy(mixT[:, j, :], bank[4 + j % 2][:, 0:S]).then_inc(o_c, 1)

            def pool_mix(g):
                w = win[g % 2]
                dve.wait_ge(win_add, (g + 1) * (g + 2) // 2)
                v.tensor_tensor(w[:, 16:32], w[:, 16:32], edge[:, g, :], ALU.mult).then_inc(win_out, 1)
                dve.wait_ge(win_out, g + 1)
                v.scalar_tensor_tensor(out=uT[:, g, 16:16 + S], in0=w[:, 16:16 + S],
                                       scalar=1.0 / WINDOWS[g], in1=uT[:, g, 16:16 + S],
                                       op0=ALU.mult, op1=ALU.subtract).then_inc(mix_ok, 1)

            dve.wait_ge(consts, 9)
            dve.wait_ge(edge_c, 15)
            softplus_head(0)
            for j in range(NPAIR):
                if j + 1 < NPAIR:
                    softplus_head(j + 1)
                weights_mask(j)
                pool_mix(j)
                if j >= 1:
                    heads_out(j - 1)
            heads_out(NPAIR - 1)
            for g in range(NG):
                dve.wait_ge(pool_ok, g // 2 + 1)
                v.tensor_scalar(mixT[:, 4 + g, :], bank[4 + g // 2][:, (g % 2) * S:(g % 2 + 1) * S],
                                PSC[:, g:g + 1], None, ALU.mult).then_inc(poolT_ok, 1)
            for b in range(2):
                r = lw[b][:].rearrange("p a b -> p (a b)")[:, 0:HALF]
                dve.wait_ge(hs_rt, b + 1)
                v.reciprocal(r, r).then_inc(hs_inv, 1)
                dve.wait_ge(hs_inv, b + 1)
                for j in (2 * b, 2 * b + 1):
                    v.scalar_tensor_tensor(out=mixT[:, j, :], in0=mixT[:, j, :],
                                           scalar=SBG[:, j:j + 1], in1=r[:, (j % 2) * S:(j % 2 + 1) * S],
                                           op0=ALU.mult, op1=ALU.mult).then_inc(sbn, 1)
            dve.wait_ge(wo_ok, 1)
            for tt in range(TT):
                for hf in range(2):
                    v.tensor_tensor(xres[:, tt, hf * HALF:(hf + 1) * HALF],
                                    xres[:, tt, hf * HALF:(hf + 1) * HALF], bank[2 * tt + hf][:],
                                    ALU.add).then_inc(x2_ok, 1)
            normalise(2, 6, 4)
            gained(4, h2T, G2)

            dve.wait_ge(lg_ok, 1)
            v.tensor_copy(lg[:, :, 0:NE], bank[0][:, 0:TT * NE].rearrange("p (a e) -> p a e", a=TT)
                          ).then_inc(lg_c, 1)
            dve.wait_ge(lg_c, 1)
            for tt in range(TT):
                v.max(out=top8[:, tt, :], in_=lg[:, tt, 0:NE]).then_inc(mx, 1)
            dve.wait_ge(mx, 2)
            v.tensor_scalar(negtop[:], top8[:, :, 0], -1.0, None, ALU.mult).then_inc(ntop, 1)
            v.memset(top8[:, :, TOP_K:8], SENTINEL).then_inc(t8, 1)
            dve.wait_ge(t8, 1)
            for tt in range(TT):
                v.match_replace(out=lgr[:, tt, :], in_to_replace=top8[:, tt, :],
                                in_values=lg[:, tt, :], imm_value=TAKEN).then_inc(mr, 1)
            dve.wait_ge(mr, 2)
            v.tensor_scalar(mask[:], lgr[:, :, 0:NE], TAKEN, None, ALU.is_ge).then_inc(mask_ok, 1)
            dve.wait_ge(mask_ok, 1)
            dve.wait_ge(ex_ok, 2)
            v.tensor_tensor(exm[:], ex[:], mask[:], ALU.mult).then_inc(exm_ok, 1)
            dve.wait_ge(exm_ok, 1)
            v.reduce_sum(stat[:, 12:14], exm[:], AX_X).then_inc(den, 1)
            dve.wait_ge(den, 1)
            v.reciprocal(stat[:, 14:16], stat[:, 12:14]).then_inc(den, 1)
            dve.wait_ge(den, 2)
            for tt in range(TT):
                v.tensor_scalar(gate[:, tt, :], exm[:, tt, :], stat[:, 14 + tt:15 + tt], None,
                                ALU.mult).then_inc(gate_ok, 1)
            dve.wait_ge(rank_ok, 1)
            v.scalar_tensor_tensor(out=rank[:, :, 0:NE],
                                   in0=bank[1][:, 0:TT * NE].rearrange("p (a e) -> p a e", a=TT),
                                   scalar=1.0, in1=mask[:], op0=ALU.add,
                                   op1=ALU.mult).then_inc(rank_p, 1)
            v.reduce_max(most[:, 0:1], bank[1][0:1, TT * NE:(TT + 1) * NE], AX_X).then_inc(cnt_m, 1)
            dve.wait_ge(rank_p, 1)
            v.tensor_scalar(rank[:, :, 0:NE], rank[:, :, 0:NE], -1.0, None, ALU.add).then_inc(
                rank_c, 1)
            dve.wait_ge(cnt_m, 1)
            v.tensor_scalar(flag[:], most[:, 0:1], float(SLOTS), None, ALU.is_gt).then_inc(flag_ok, 1)
            dve.wait_ge(gate_ok, 2)
            dve.wait_ge(pool_c, 7)
            for tt in range(TT):
                v.tensor_copy(gtab[:, tt, 0:NE // 2, 0:2],
                              gate[:, tt, :].rearrange("p (q r) -> p q r", r=2)).then_inc(gtab_ok, 1)
            dve.wait_ge(gT_ok, 1)
            v.tensor_copy(gateT[:], bank[2][0:NE, 0:S]).then_inc(gT_c, 1)
            dve.wait_ge(rank_c, 1)

            dve.wait_ge(flag_ok, 1)
            crowded = dve.value_load(flag[0:1, 0:1], min_val=0, max_val=1)

            def pick_rows(q, p):
                for tt in range(TT):
                    for r in range(2):
                        d = v.tensor_scalar(pick[p][:, tt, r * SLOTS:(r + 1) * SLOTS],
                                            iota[:, 0:SLOTS], rank[:, tt, bass.ds(2 * q + r, 1)], None,
                                            ALU.is_equal)
                d.then_inc(pick_ok, 1)

            def scatter_matrix(q, p):
                dve.wait_ge(info_ok, q + 1)
                v.tensor_copy(info[:], BM[:, 0:3]).then_inc(info_c, 1)
                dve.wait_ge(info_c, q + 1)
                for r in range(2):
                    lo = r * SLOTS
                    d = v.tensor_scalar(scat[p][lo:lo + SLOTS, :], iota[lo:lo + SLOTS, :],
                                        info[lo:lo + SLOTS, 2:3], info[lo:lo + SLOTS, r:r + 1],
                                        ALU.is_equal, ALU.mult)
                d.then_inc(scat_ok, 1)

            def gathered(q, p, kh, ready, done):
                dve.wait_ge(ready, q + 1)
                v.tensor_tensor(xT[p][:, 4 * kh:4 * kh + 4, :],
                                BM[:].rearrange("p (k t) -> p k t", k=4),
                                G2[:, 4 * kh:4 * kh + 4].unsqueeze(2).to_broadcast([P, 4, P]),
                                ALU.mult).then_inc(done, 1)

            def swiglu(n, ready, gbank, ubank, gc, uc, sg, tm, hh):
                dve.wait_ge(ready[0], ready[1])
                v.tensor_scalar(gatec, gbank[:], LIMIT, None, ALU.min).then_inc(gc, 1)
                v.tensor_scalar(upc, ubank[:], LIMIT, -LIMIT, ALU.min, ALU.max).then_inc(uc, 1)
                dve.wait_ge(gc, n)
                dve.wait_ge(uc, n)
                v.scalar_tensor_tensor(out=act_t, in0=upc, scalar=1.0, in1=gatec, op0=ALU.add,
                                       op1=ALU.mult).then_inc(tm, 1)
                dve.wait_ge(tm, n)
                dve.wait_ge(sg, n)
                v.tensor_tensor(act_h, act_t, sig, ALU.mult).then_inc(hh, 1)

            def rows_out(e, r):
                dve.wait_ge(chunks_used, (e + 1) * PER_EXPERT)
                lo = (r % 2) * SLOTS
                v.tensor_copy(ypair[lo:lo + SLOTS, HALF:D], BY[SLOTS:P, :]).then_inc(y_hi, 1)

            def fast_pair(q, p):
                pick_rows(q + 1, 1 - p)
                swiglu(2 * q + 1, (chunks_used, q * (2 * PER_EXPERT) + UP_CHUNKS), BG, BU, gc_ok, uc_ok, sig_ok, t_ok, h_ok)
                scatter_matrix(q + 1, 1 - p)
                rows_out(2 * q, 0)
                swiglu(2 * q + 2, (chunks_used, q * (2 * PER_EXPERT) + (PER_EXPERT + UP_CHUNKS)), BG, BU, gc_ok, uc_ok, sig_ok, t_ok, h_ok)
                gathered(q + 1, 1 - p, 0, ga_ok, xa_ok)
                gathered(q + 1, 1 - p, 1, gb_ok, xb_ok)
                rows_out(2 * q + 1, 1)

            with dve.If(crowded):
                dve.wait_ge(bd_ok, 1)
                for tt in range(TT):
                    for hf in range(2):
                        v.tensor_copy(xn[:, tt, hf * HALF:(hf + 1) * HALF],
                                      bank[2 * tt + hf][:]).then_inc(n_acc0, 1)
                with dve.Fori(0, NE) as e:
                    for tt in range(TT):
                        for hf in range(2):
                            swiglu(e * 4 + (2 * tt + hf + 1), (n_up, e * 2 + (tt + 1)), bank[hf],
                                   bank[2 + hf], n_gc, n_uc, n_sig, n_t, n_h)
                        if tt == 0:
                            dve.wait_ge(n_y, e + 1)
                        else:
                            dve.wait_ge(chunks_used, (e + 1) * PER_EXPERT)
                        if tt == 0:
                            dve.wait_ge(n_acc0, 4)
                        dve.wait_ge(n_acc, e * 4 + 2 * tt)
                        for hf in range(2):
                            v.scalar_tensor_tensor(
                                out=xn[:, tt, hf * HALF:(hf + 1) * HALF], in0=bank[5 + hf][:],
                                scalar=gate[:, tt, bass.ds(e, 1)],
                                in1=xn[:, tt, hf * HALF:(hf + 1) * HALF], op0=ALU.mult,
                                op1=ALU.add).then_inc(n_acc, 1)
                dve.wait_ge(n_acc, 4 * NE)
                for tt in range(TT):
                    for hf in range(2):
                        v.tensor_tensor(xres[:, tt, hf * HALF:(hf + 1) * HALF],
                                        xres[:, tt, hf * HALF:(hf + 1) * HALF],
                                        xn[:, tt, hf * HALF:(hf + 1) * HALF],
                                        ALU.add).then_inc(sum_ok, 1)
            with dve.Else():
                pick_rows(0, 0)
                scatter_matrix(0, 0)
                gathered(0, 0, 0, ga_ok, xa_ok)
                gathered(0, 0, 1, gb_ok, xb_ok)
                with dve.Fori(0, NE // BODY) as i:
                    for p in range(2):
                        fast_pair(i * 2 + p, p)
                dve.wait_ge(comb_ok, NE // 2)
                for tt in range(TT):
                    for hf in range(2):
                        v.tensor_tensor(xres[:, tt, hf * HALF:(hf + 1) * HALF],
                                        xres[:, tt, hf * HALF:(hf + 1) * HALF],
                                        bank[2 * tt + hf][:], ALU.add).then_inc(sum_ok, 1)

            dve.wait_ge(fg_in, 16)
            for tt in range(TT):
                dve.wait_ge(frt, tt + 1)
                v.reciprocal(stat[:, 10 + tt:11 + tt], stat[:, 10 + tt:11 + tt]).then_inc(finv, 1)
                dve.wait_ge(finv, tt + 1)
                v.scalar_tensor_tensor(out=xn[:, tt, :], in0=xres[:, tt, :],
                                       scalar=stat[:, 10 + tt:11 + tt], in1=wide[:], op0=ALU.mult,
                                       op1=ALU.mult).then_inc(fin, 1)

        @block.tensor
        def _(pe):
            t = nc.tensor

            def mm(o, l, r, start=False, stop=False):
                return t.matmul(o, l, r, start=start, stop=stop, skip_group_check=True)

            for i in range(4):
                pe.wait_ge(vecs_in[i], 16)
            pe.wait_ge(consts, 9)
            t.transpose(bank[7][:, 0:24], vecs[:], ident[0:24, 0:24]).then_inc(vec_t, 1)

            def turn(first, base):
                for n in range(4):
                    tt, kh = n // 2, n % 2
                    pe.wait_ge(xn_ok, base + tt + 1)
                    for k in range(4):
                        m = t.transpose(bank[first + n][:, k * P:(k + 1) * P],
                                        xn[:, tt, (4 * kh + k) * P:(4 * kh + k + 1) * P], ident[:])
                    m.then_inc(tr, 1)

            turn(0, 0)
            pe.wait_ge(tr_c, 4)
            pe.wait_ge(vec_c, 1)
            for k in range(KD):
                pe.wait_ge(win_in[k], 16)
                w = ring[:, k * CHUNK:(k + 1) * CHUNK]
                for m in range(12):
                    col = m * P if m < 8 else 3 * SBW + (m - 8) * P
                    mm(bank[m // 2][:, (m % 2) * S:(m % 2 + 1) * S], w[:, col:col + P], hT[:, k, :],
                       start=(k == 0 and m % 2 == 0), stop=(k == KD - 1 and m % 2 == 1))
                for tt in range(TT):
                    z = mm(bank[6 + tt][:], hT[:, k, tt * P:(tt + 1) * P], w[:, 2 * SBW:3 * SBW],
                           start=(k == 0), stop=(k == KD - 1))
                if k == KD - 1:
                    z.then_inc(proj, 1)
            pe.wait_ge(q_c, 2)
            pe.wait_ge(k_c, 2)

            def scores(j):
                if j >= 2:
                    pe.wait_ge(a_exp, 2 * j - 2)
                for h in range(2):
                    zb = bank[2 * (j % 2) + h]
                    q = qkT[h * HD:(h + 1) * HD, j, :]
                    kk = qkT[h * HD:(h + 1) * HD, NPAIR + j, :]
                    mm(zb[:, 0:S], kk[:, 0:P], q, start=True)
                    m = mm(zb[:, S:S + P], kk[:, P:S], q[:, P:S])
                m.then_inc(z_ok, 1)

            def after_sums(j):
                pe.wait_ge(l_ok, 2 * j + 2)
                for h in range(2):
                    zb = bank[2 * (j % 2) + h]
                    lt = lw[j % 2][:, h, :]
                    mm(zb[:, 0:S], negtri[:], lt[:, 0:S])
                    mm(zb[:, P:S], negones[:], lt[:, S:S + P])
                    m = mm(zb[:, S:S + P], negtri[:], lt[:, S:S + P], stop=True)
                m.then_inc(zc_ok, 1)

            def values(j):
                pe.wait_ge(a_ok, 4 * j + 4)
                if j >= 2:
                    pe.wait_ge(o_c, j - 1)
                for h in range(2):
                    hd = (2 * j + h) * HD
                    ob = bank[4 + j % 2][h * HD:(h + 1) * HD, :]
                    wt = aw[j % 2][:, h, :]
                    mm(ob[:, 0:S], vtok[:, 0, hd:hd + HD], wt[:, 0:S], start=True)
                    m = mm(ob[:, P:S], vtok[:, 1, hd:hd + HD], wt[:, S:S + P], stop=True)
                m.then_inc(o_ok, 1)

            def mean_squares(j):
                pe.wait_ge(sq_ok, j + 1)
                mm(bank[6 + j // 2][:, (j % 2) * S:(j % 2 + 1) * S], headmean[:], sq[:],
                   start=(j % 2 == 0), stop=(j % 2 == 1)).then_inc(ms_ok, 1)

            pe.wait_ge(edge_c, 15)
            scores(0)
            scores(1)
            pe.wait_ge(v_c, 1)
            pe.wait_ge(v2_c, 1)
            pe.wait_ge(u_c, 1)
            for j in range(NPAIR):
                after_sums(j)
                values(j)
                if j + 2 < NPAIR:
                    scores(j + 2)
                if j >= 1:
                    mean_squares(j - 1)
            mean_squares(NPAIR - 1)
            pe.wait_ge(wpool_in, 16)
            pe.wait_ge(o_c, NPAIR)
            for g in range(NG):
                pe.wait_ge(mix_ok, g + 1)
                m = mm(bank[4 + g // 2][:, (g % 2) * S:(g % 2 + 1) * S], wpool[:, g, :],
                       uT[:, g, 16:16 + S], start=(g % 2 == 0), stop=(g % 2 == 1))
                if g % 2 == 1:
                    m.then_inc(pool_ok, 1)
            pe.wait_ge(a_exp, 2 * NPAIR)
            for n, k in enumerate((4, 5, 6, 7, 0, 1, 2, 3)):
                pe.wait_ge(wout_in[k // 2], 16)
                if k >= 4:
                    pe.wait_ge(poolT_ok, k - 3)
                else:
                    pe.wait_ge(sbn, k + 1)
                for tt in range(TT):
                    for hf in range(2):
                        lo = (8 + k // 2) * CHUNK + (k % 2) * D + hf * HALF
                        m = mm(bank[2 * tt + hf][:], mixT[:, k, tt * P:(tt + 1) * P],
                               ring[:, lo:lo + HALF], start=(n == 0), stop=(n == KD - 1))
            m.then_inc(wo_ok, 1)

            turn(4, 2)
            pe.wait_ge(x2_ok, 4)
            pe.wait_ge(wrouter_in, 16)
            pe.wait_ge(brow_in, 16)
            pe.wait_ge(tr_c, 8)
            for tt in range(TT):
                lo = bank[0][:, tt * NE:(tt + 1) * NE]
                mm(lo, ones[0:1, :], brow[:], start=(tt == 0))
                for k in range(KD):
                    m = mm(lo, h2T[:, k, tt * P:(tt + 1) * P], wrouter[:, k, :],
                           stop=(k == KD - 1 and tt == 1))
            m.then_inc(lg_ok, 1)
            pe.wait_ge(mask_ok, 1)
            mm(bank[1][:, 0:NE], before[:], mask[:, 0, :], start=True)
            mm(bank[1][:, NE:2 * NE], before[:], mask[:, 1, :])
            mm(bank[1][:, NE:2 * NE], ones[:], mask[:, 0, :])
            mm(bank[1][:, 2 * NE:3 * NE], ones[:], mask[:, 0, :])
            mm(bank[1][:, 2 * NE:3 * NE], ones[:], mask[:, 1, :], stop=True).then_inc(rank_ok, 1)
            pe.wait_ge(gate_ok, 2)
            for tt in range(TT):
                m = t.transpose(bank[2][0:NE, tt * P:(tt + 1) * P], gate[:, tt, :], ident[:])
            m.then_inc(gT_ok, 1)
            pe.wait_ge(bdown_in, 16)
            pe.wait_ge(gT_c, 1)
            pe.wait_ge(rank_c, 1)
            pe.wait_ge(flag_ok, 1)
            for tt in range(TT):
                for hf in range(2):
                    m = mm(bank[2 * tt + hf][:], gateT[:, tt * P:(tt + 1) * P],
                           wide[0:NE, hf * HALF:(hf + 1) * HALF], start=True)
            m.then_inc(bd_ok, 1)

            crowded = pe.value_load(flag[0:1, 0:1], min_val=0, max_val=1)

            def chunk_wait(i, m):
                pe.wait_ge(chunk_in[slot_of(m)], i * (16 * GEN) + 16 * (m // RING + 1))

            def slot_info(q, p):
                pe.wait_ge(pick_ok, q + 1)
                for tt in range(TT):
                    m = mm(BM[:, 0:3], pick[p][:, tt, :], gtab[:, tt, bass.ds(q, 1), :].rearrange(
                        "p a b -> p (a b)"), start=(tt == 0), stop=(tt == 1))
                m.then_inc(info_ok, 1)

            def gather(q, p, kh, free, done):
                pe.wait_ge(free, q + 1)
                for k in range(4):
                    f = (4 * kh + k) * P
                    for tt in range(TT):
                        m = mm(BM[:, k * P:(k + 1) * P], xn[:, tt, f:f + P], pick[p][:, tt, :],
                               start=(k == 0 and tt == 0), stop=(k == 3 and tt == 1))
                m.then_inc(done, 1)

            def combine(q, p):
                pe.wait_ge(scat_ok, q + 1)
                pe.wait_ge(y_lo, 2 * q + 2)
                pe.wait_ge(y_hi, 2 * q + 2)
                for tt in range(TT):
                    for hf in range(2):
                        m = mm(bank[2 * tt + hf][:], scat[p][:, tt * P:(tt + 1) * P],
                               ypair[:, hf * HALF:(hf + 1) * HALF])
                m.then_inc(comb_ok, 1)

            def fast_expert(i, r, q, p, not_first):
                e = 2 * q + r % 2
                m0 = r * PER_EXPERT
                cols = slice((r % 2) * SLOTS, (r % 2 + 1) * SLOTS)
                pe.wait_ge(bias_in[r % 2], i * 32 + 16 * (r // 2 + 1))
                mm(BG[:], bsel[:, 0, :], bias[:, r % 2, :], start=True)
                mm(BU[:], bsel[:, 1, :], bias[:, r % 2, :], start=True).then_inc(bias_used, 1)
                if r % 2 == 0:
                    pe.wait_ge(xb_ok, q + 1)
                for k in range(KD):
                    chunk_wait(i, m0 + k)
                    for gu, b in ((0, BG), (1, BU)):
                        for hf in range(2):
                            m = mm(b[hf * SLOTS:(hf + 1) * SLOTS, :], xT[p][:, k, cols],
                                   up_w(m0 + k, gu, hf), stop=(k == KD - 1))
                    m.then_inc(chunks_used, 1)
                if r % 2 == 0:
                    if not_first:
                        combine(q - 1, 1 - p)
                else:
                    gather(q + 1, 1 - p, 0, info_c, ga_ok)
                pe.wait_ge(h_ok, e + 1)
                for j in range(4):
                    m = t.transpose(BG[:, j * P:(j + 1) * P], act_h[:, j * P:(j + 1) * P], ident[:])
                m.then_inc(hT_ok, 1)
                if r % 2 == 0:
                    slot_info(q + 1, 1 - p)
                else:
                    gather(q + 1, 1 - p, 1, xa_ok, gb_ok)
                pe.wait_ge(hT_c, e + 1)
                for c in range(DOWN_CHUNKS):
                    n = m0 + UP_CHUNKS + c
                    chunk_wait(i, n)
                    for s in range(2):
                        f = 2 * c + s
                        half, j = f // 4, f % 4
                        for hf in range(2):
                            m = mm(BY[hf * SLOTS:(hf + 1) * SLOTS, :],
                                   hidT[:, j, half * SLOTS:(half + 1) * SLOTS], down_w(n, s, hf),
                                   start=(f == 0), stop=(f == KF - 1))
                    m.then_inc(chunks_used, 1)

            def fast_body(i, first):
                for r in range(BODY):
                    q = i * 2 + r // 2
                    fast_expert(i, r, q, r // 2, not (first and r < 2))

            with pe.If(crowded):
                pe.wait_ge(n_acc0, 4)

                def all_tokens(i, r):
                    e = i * BODY + r
                    m0 = r * PER_EXPERT
                    pe.wait_ge(bias_in[r % 2], i * 32 + 16 * (r // 2 + 1))
                    for tt in range(TT):
                        for b in range(4):
                            m = mm(bank[b][:], bsel[:, 2 + b, :], bias[:, r % 2, :], start=True)
                        if tt == TT - 1:
                            m.then_inc(bias_used, 1)
                        for k in range(KD):
                            if tt == 0:
                                chunk_wait(i, m0 + k)
                            for b in range(4):
                                m = mm(bank[b][:], h2T[:, k, tt * P:(tt + 1) * P],
                                       up_w(m0 + k, b // 2, b % 2), stop=(k == KD - 1))
                        m.then_inc(n_up, 1)
                        for hf in range(2):
                            n = e * 4 + (2 * tt + hf + 1)
                            pe.wait_ge(n_h, n)
                            if hf == 1:
                                pe.wait_ge(n_hTc, e * 4 + (2 * tt + 1))
                            for j in range(4):
                                m = t.transpose(BG[:, j * P:(j + 1) * P],
                                                act_h[:, j * P:(j + 1) * P], ident[:])
                            m.then_inc(n_hT, 1)
                        pe.wait_ge(n_hTc, e * 4 + (2 * tt + 2))
                        pe.wait_ge(n_acc, e * 4 + 2 * tt)
                        for f in range(KF):
                            n = m0 + UP_CHUNKS + f // 2
                            if tt == 0 and f % 2 == 0:
                                chunk_wait(i, n)
                            for hf in range(2):
                                m = mm(bank[5 + hf][:], hidT_all[:, f, :], down_w(n, f % 2, hf),
                                       start=(f == 0), stop=(f == KF - 1))
                        if tt == 0:
                            m.then_inc(n_y, 1)
                        else:
                            m.then_inc(chunks_used, PER_EXPERT)

                with pe.Fori(0, NBODY) as i:
                    for r in range(BODY):
                        all_tokens(i, r)
            with pe.Else():
                pe.wait_ge(gtab_ok, 2)
                slot_info(0, 0)
                gather(0, 0, 0, info_c, ga_ok)
                gather(0, 0, 1, xa_ok, gb_ok)
                fast_body(0, True)
                with pe.Fori(1, NBODY) as i:
                    fast_body(i, False)
                combine(NE // 2 - 1, 1)


_INS = ["x", "norm1_g", "w_in", "sb_norm_g", "w_pool", "pool_scale", "w_out", "norm2_g", "w_router",
        "b_router", "w_gate_up", "b_gate_up", "w_down", "b_down", "final_norm_g"]


def kernel(**inputs):
    import numpy as _np
    import concourse.bacc as _bacc
    from concourse import mybir as _mybir
    from concourse.bass_utils import run_bass_kernel_spmd as _run

    nc = _bacc.Bacc("TRN2", target_bir_lowering=False, num_devices=1)
    arrays, args = {}, []
    for name in _INS:
        a = _np.ascontiguousarray(inputs[name])
        arrays[f"in_{name}_dram"] = a
        args.append(nc.dram_tensor(f"in_{name}_dram", a.shape, _mybir.dt.from_np(a.dtype),
                                   kind="ExternalInput").ap())
    shape = tuple(inputs["x"].shape)
    args.append(nc.dram_tensor("out_0_dram", shape, _mybir.dt.float32, kind="ExternalOutput").ap())
    build(nc, *args)
    r = _run(nc, [arrays], core_ids=[0])
    return r.results[0]["out_0_dram"]
```

```python
from contextlib import ExitStack

import concourse.bass as bass
from concourse import mybir

F32 = mybir.dt.float32
I32 = mybir.dt.int32
ALU = mybir.AluOpType
ACT = mybir.ActivationFunctionType
AX_X = mybir.AxisListType.X

P = 128
EPS = 1e-5
TOP_K = 4
WINDOWS = (2, 4, 8, 16)
LIMIT = 7.0
ALPHA = 1.702
SLOTS = 64
SENTINEL = 2.0e38
TAKEN = 3.0e38


def build(nc, x, norm1_g, w_in, sb_norm_g, w_pool, pool_scale, w_out, norm2_g, w_router, b_router,
          w_gate_up, b_gate_up, w_down, b_down, final_norm_g, out):
    _, S, D = x.shape
    NIN = w_in.shape[2]
    _, NE, _, F2 = w_gate_up.shape
    F = F2 // 2
    SBW = sb_norm_g.shape[1]
    _, NG, GC, _ = w_pool.shape
    HD = 64
    TT = S // P
    KD = D // P
    KF = F // P
    NPAIR = SBW // P
    HALF = 512
    assert (S, D, F, NIN, NE, SBW, NG, GC) == (256, 1024, 1024, 2048, 32, 512, 4, 128)

    CHUNK = 2048
    RING = 16
    UP_CHUNKS = KD
    DOWN_CHUNKS = KF // 2
    PER_EXPERT = UP_CHUNKS + DOWN_CHUNKS
    BODY = 4
    NBODY = NE // BODY
    PER_BODY = BODY * PER_EXPERT
    GEN = PER_BODY // RING
    FIRST_SLOT = RING - 4
    assert PER_BODY % RING == 0 and UP_CHUNKS == 8 and DOWN_CHUNKS == 4

    def slot_of(n):
        return (FIRST_SLOT + n) % RING

    rows = {
        "wgu": w_gate_up.rearrange("l e d f -> (l e d) f"),
        "wd": w_down.rearrange("l e f d -> (l e f) d"),
        "bgu": b_gate_up.rearrange("l e (r c) -> (l e r) c", c=HALF),
    }

    with ExitStack() as ctx:
        def sb(name, shape, dt=F32):
            return ctx.enter_context(nc.sbuf_tensor(name, shape, dt))

        def sem(name):
            return ctx.enter_context(nc.semaphore(name))

        ring = sb("ring", [P, RING * CHUNK])
        w_qk = ring[:, 0:4 * CHUNK].rearrange("p (k n) -> p k n", k=KD)
        w_v = ring[:, 4 * CHUNK:6 * CHUNK].rearrange("p (k n) -> p k n", k=KD)
        w_u = ring[:, 6 * CHUNK:8 * CHUNK].rearrange("p (k n) -> p k n", k=KD)
        w_o = ring[:, 8 * CHUNK:12 * CHUNK].rearrange("p (k n) -> p k n", k=KD)
        WO_ROWS = (4, 6, 0, 2)
        xres = sb("xres", [P, TT, D])
        xn = sb("xn", [P, TT, D])
        area = sb("area", [P, 10240])

        def part(lo, n, a=None):
            v = area[:, lo:lo + n]
            return v if a is None else v.rearrange("p (a b) -> p a b", a=a)

        hT = part(0, KD * S, KD)
        mixT = [xn[:, 1, S * j:S * (j + 1)] for j in range(4)] + [part(S * j, S) for j in range(4)]
        qkT = part(2048, 2048, 8)
        vtok = part(4096, TT * SBW, TT)
        uT = part(5120, NG * (S + 16), NG)
        lw = [part(6208 + 768 * i, 768, 2) for i in range(2)]
        aw = [part(7744 + 768 * i, 768, 2) for i in range(2)]
        win = [part(9280 + 272 * i, 272) for i in range(2)]
        sq = part(9824, S)
        h2T = part(0, KD * S, KD)
        xT = [part(2048 + 1024 * i, 1024, KD) for i in range(2)]
        gatec, upc, sig, act_t, act_h = [part(4096 + HALF * i, HALF) for i in range(5)]
        hidT = part(6656, HALF, 4)
        ypair = part(7168, D)
        scat = [part(8192 + S * i, S) for i in range(2)]
        pick = [part(8704 + 2 * P * i, 2 * P, TT) for i in range(2)]
        hidT_all = part(2048, 1024, KF)

        wide = sb("wide", [P, D])
        wpool = sb("wpool", [P, NG, GC])
        wrouter = sb("wrouter", [P, KD, NE])
        brow = sb("brow", [P, NE])
        bias = sb("bias", [4, 2, HALF])
        bsel = sb("bsel", [4, 6, P])
        vecs = sb("vecs", [24, P])
        vecT = sb("vecT", [P, 24])
        ident = sb("ident", [P, P])
        negtri = sb("negtri", [P, P])
        negones = sb("negones", [P, P])
        ones = sb("ones", [P, P])
        before = sb("before", [P, P])
        headmean = sb("headmean", [P, P])
        iota_i = sb("iota_i", [P, S], I32)
        iota = sb("iota", [P, S])
        edge = sb("edge", [P, NG, 16])
        lg = sb("lg", [P, TT, NE + 4])
        lgr = sb("lgr", [P, TT, NE + 4])
        top8 = sb("top8", [P, TT, 8])
        negtop = sb("negtop", [P, TT])
        mask = sb("mask", [P, TT, NE])
        ex = sb("ex", [P, TT, NE])
        exm = sb("exm", [P, TT, NE])
        gate = sb("gate", [P, TT, NE])
        gateT = sb("gateT", [NE, S])
        rank = sb("rank", [P, TT, NE + 2])
        gtab = sb("gtab", [P, TT, NE // 2 + 1, 3])
        info = sb("info", [P, 3])
        stat = sb("stat", [P, 16])
        epsc = sb("epsc", [P, 1])
        most = sb("most", [1, 2])
        flag = sb("flag", [1, 1], I32)
        bank = [ctx.enter_context(nc.psum_tensor(f"bank{i}", [P, HALF], F32)) for i in range(8)]
        G1, G2, SBG, PSC = vecT[:, 0:8], vecT[:, 8:16], vecT[:, 16:20], vecT[:, 20:24]
        BG, BU, BY, BM = bank[4], bank[5], bank[6], bank[7]

        x_in = [sem(f"x_in{i}") for i in range(TT)]
        vecs_in = [sem(f"vecs_in{i}") for i in range(4)]
        wpool_in, wrouter_in, brow_in, bdown_in, fg_in = map(
            sem, ("wpool_in", "wrouter_in", "brow_in", "bdown_in", "fg_in"))
        wqk_in = [sem(f"wqk_in{i}") for i in range(8)]
        wv_in = [sem(f"wv_in{i}") for i in range(2)]
        wu_in = [sem(f"wu_in{i}") for i in range(2)]
        wout_in = [sem(f"wout_in{i}") for i in range(4)]
        chunk_in = [sem(f"chunk_in{i}") for i in range(RING)]
        bias_in = [sem(f"bias_in{i}") for i in range(2)]
        chunks_used = sem("chunks_used")
        bias_used = sem("bias_used")
        out_done = sem("out_done")

        consts, pool_c, iota_f, edge_c = map(sem, ("consts", "pool_c", "iota_f", "edge_c"))
        vec_t, vec_c = sem("vec_t"), sem("vec_c")
        ssq1 = sem("ssq1")
        warm = sem("warm")
        ssq, rtd, rinv, xn_ok = map(sem, ("ssq", "rtd", "rinv", "xn_ok"))
        tr, tr_c = sem("tr"), sem("tr_c")
        qk_ok, v_ok, u_ok, wo_half = map(sem, ("qk_ok", "v_ok", "u_ok", "wo_half"))
        q_c, k_c, v_c, v2_c, u_c = map(sem, ("q_c", "k_c", "v_c", "v2_c", "u_c"))
        win_add, win_out, mix_ok = map(sem, ("win_add", "win_out", "mix_ok"))
        z_ok, t1, t2, t3, l_add, l_ok, zc_ok, a_exp, a_ok, o_ok, o_c, sq_ok, ms_ok = map(
            sem, ("z_ok", "t1", "t2", "t3", "l_add", "l_ok", "zc_ok", "a_exp", "a_ok", "o_ok", "o_c",
                  "sq_ok", "ms_ok"))
        hs_rt, hs_inv, sbn = map(sem, ("hs_rt", "hs_inv", "sbn"))
        pool_ok, poolT_ok = sem("pool_ok"), sem("poolT_ok")
        wo_ok, x2_ok = sem("wo_ok"), sem("x2_ok")
        lg_ok, lg_c, mx, ntop, t8, mr, mask_ok, ex_ok, exm_ok, den, gate_ok = map(
            sem, ("lg_ok", "lg_c", "mx", "ntop", "t8", "mr", "mask_ok", "ex_ok", "exm_ok", "den",
                  "gate_ok"))
        rank_ok, rank_p, rank_c, cnt_m, flag_ok, gtab_ok, gT_ok, gT_c, bd_ok = map(
            sem, ("rank_ok", "rank_p", "rank_c", "cnt_m", "flag_ok", "gtab_ok", "gT_ok", "gT_c",
                  "bd_ok"))
        pick_ok, info_ok, info_c, scat_ok, ga_ok, gb_ok, xa_ok, xb_ok = map(
            sem, ("pick_ok", "info_ok", "info_c", "scat_ok", "ga_ok", "gb_ok", "xa_ok", "xb_ok"))
        gc_ok, uc_ok, sig_ok, t_ok, h_ok, hT_ok, hT_c, y_lo, y_hi, comb_ok = map(
            sem, ("gc_ok", "uc_ok", "sig_ok", "t_ok", "h_ok", "hT_ok", "hT_c",
                  "y_lo", "y_hi", "comb_ok"))
        n_up, n_gc, n_uc, n_sig, n_t, n_h, n_hT, n_hTc, n_y, n_acc = map(
            sem, ("n_up", "n_gc", "n_uc", "n_sig", "n_t", "n_h", "n_hT", "n_hTc", "n_y",
                  "n_acc"))
        last_ok, sum_ok, fsq, fadd, frt, finv, fin = map(
            sem, ("last_ok", "sum_ok", "fsq", "fadd", "frt", "finv", "fin"))

        def up_w(n, gu, half):
            lo = slot_of(n) * CHUNK + gu * F + half * HALF
            return ring[:, lo:lo + HALF]

        def down_w(n, s, half):
            lo = slot_of(n) * CHUNK + s * D + half * HALF
            return ring[:, lo:lo + HALF]

        block = ctx.enter_context(nc.Block())

        @block.sync
        def _(sp):
            for tt in range(TT):
                sp.dma_start(xres[:, tt, :], x[0, tt * P:(tt + 1) * P, :]).then_inc(x_in[tt], 16)
            for k in range(KD):
                sp.dma_start(w_qk[:, k, :], w_in[0, k * P:(k + 1) * P, 0:2 * SBW]).then_inc(
                    wqk_in[k], 16)
            for w, col, done in ((w_v, 2 * SBW, wv_in), (w_u, 3 * SBW, wu_in)):
                for c in range(2):
                    sp.dma_start(w[:, 4 * c:4 * c + 4, :],
                                 w_in[0, c * HALF:(c + 1) * HALF, col:col + SBW].rearrange(
                                     "(k p) n -> p k n", p=P)).then_inc(done[c], 16)
            for c in range(4):
                row = WO_ROWS[c] * P
                sp.dma_start(w_o[:, 2 * c:2 * c + 2, :],
                             w_out[0, row:row + 2 * P, :].rearrange("(s p) n -> p s n", s=2)
                             ).then_inc(wout_in[c], 16)

            def load_expert(e, m0, first):
                r = m0 // PER_EXPERT
                if not first or r >= 2:
                    sp.wait_ge(bias_used, e - 1)
                sp.dma_start(bias[:, r % 2, :], rows["bgu"][bass.ds(e * 4, 4), :]).then_inc(
                    bias_in[r % 2], 16)
                if first and r == 2:
                    sp.wait_ge(bd_ok, 1)
                    sp.dma_start(wide[:], final_norm_g.rearrange("(a d) -> a d", a=1).broadcast_to(
                        [P, D])).then_inc(fg_in, 16)
                for c in range(PER_EXPERT):
                    m = m0 + c
                    s = slot_of(m)
                    n = e * PER_EXPERT + c
                    if first and m < RING:
                        if 4 <= m < 8:
                            sp.wait_ge(qk_ok, 1)
                        elif 8 <= m < 10:
                            sp.wait_ge(v_ok, 1)
                        elif 10 <= m < 12:
                            sp.wait_ge(u_ok, 2)
                        elif 12 <= m < 14:
                            sp.wait_ge(wo_half, 1)
                        elif m >= 14:
                            sp.wait_ge(wo_ok, 2)
                    else:
                        sp.wait_ge(chunks_used, n - (RING - 1))
                    dst = ring[:, s * CHUNK:(s + 1) * CHUNK]
                    if c < UP_CHUNKS:
                        src = rows["wgu"][bass.ds(e * D + c * P, P), :]
                    else:
                        src = rows["wd"][bass.ds(e * F + (c - UP_CHUNKS) * 2 * P, 2 * P), :].rearrange(
                            "(s p) n -> p s n", s=2)
                        dst = dst.rearrange("p (s n) -> p s n", s=2)
                    sp.dma_start(dst, src).then_inc(chunk_in[s], 16)

            for r in range(BODY):
                load_expert(r, r * PER_EXPERT, True)
            with sp.Fori(1, NBODY) as i:
                for r in range(BODY):
                    load_expert(i * BODY + r, r * PER_EXPERT, False)
            for n in range(4):
                tt, c = n // 2, (n % 2) * HALF
                sp.wait_ge(fin, n + 1)
                sp.dma_start(out[0, tt * P:(tt + 1) * P, c:c + HALF],
                             xn[:, tt, c:c + HALF]).then_inc(out_done, 16)
            sp.wait_ge(out_done, 64)

        @block.gpsimd
        def _(pool):
            g = nc.gpsimd
            g.memset(ident[:], 0.0).then_inc(pool_c, 1)
            g.memset(negtri[:], -1.0).then_inc(pool_c, 1)
            g.memset(before[:], 1.0).then_inc(pool_c, 1)
            g.memset(bsel[:], 0.0).then_inc(pool_c, 1)
            pool.wait_ge(pool_c, 4)
            g.affine_select(ident[:], ident[:], compare_op=ALU.not_equal, fill=1.0, base=0,
                            pattern=[[-1, P]], channel_multiplier=1).then_inc(consts, 1)
            g.affine_select(negtri[:], negtri[:], compare_op=ALU.is_ge, fill=0.0, base=0,
                            pattern=[[-1, P]], channel_multiplier=1).then_inc(consts, 1)
            g.affine_select(before[:], before[:], compare_op=ALU.is_gt, fill=0.0, base=0,
                            pattern=[[1, P]], channel_multiplier=-1).then_inc(consts, 1)
            g.affine_select(bsel[:, 0:2, 0:SLOTS], bsel[:, 0:2, 0:SLOTS], compare_op=ALU.not_equal,
                            fill=1.0, base=0, pattern=[[-2, 2], [0, SLOTS]],
                            channel_multiplier=1).then_inc(consts, 1)
            g.affine_select(bsel[:, 0:2, SLOTS:P], bsel[:, 0:2, SLOTS:P], compare_op=ALU.not_equal,
                            fill=1.0, base=-1, pattern=[[-2, 2], [0, SLOTS]],
                            channel_multiplier=1).then_inc(consts, 1)
            g.affine_select(bsel[:, 2:6, :], bsel[:, 2:6, :], compare_op=ALU.not_equal,
                            fill=1.0, base=0, pattern=[[-1, 4], [0, P]],
                            channel_multiplier=1).then_inc(consts, 1)
            g.iota(iota_i[:], pattern=[[1, S]], base=0, channel_multiplier=0).then_inc(pool_c, 1)
            for tt in range(TT):
                g.iota(gtab[:, tt, :, 2], pattern=[[0, NE // 2 + 1]], base=tt * P,
                       channel_multiplier=1,
                       allow_small_or_imprecise_dtypes=True).then_inc(pool_c, 1)
            pool.wait_ge(pool_c, 5)
            g.tensor_copy(iota[:], iota_i[:]).then_inc(iota_f, 1)
            for b in range(2):
                g.memset(win[b][:, 0:16], 0.0).then_inc(pool_c, 1)
            g.memset(uT[:, :, 0:16], 0.0).then_inc(pool_c, 1)
            pool.wait_ge(pool_c, 10)
            n = 0
            for gr in range(NG):
                pool.wait_ge(u_c, gr // 2 + 1)
                src = uT[:, gr, :]
                for lev in range(gr + 1):
                    w = 1 << lev
                    if n >= 1:
                        pool.wait_ge(win_add, n)
                    if lev == 0 and gr >= 1:
                        pool.wait_ge(mix_ok, gr)
                    dst = win[lev % 2]
                    g.tensor_tensor(dst[:, 16:16 + S], src[:, 16:16 + S], src[:, 16 - w:16 - w + S],
                                    ALU.add).then_inc(win_add, 1)
                    n += 1
                    src = dst

        @block.scalar
        def _(act):
            a = nc.scalar
            for i, (src, lo, n) in enumerate(((norm1_g, 0, 8), (norm2_g, 8, 8), (sb_norm_g, 16, 4),
                                              (pool_scale, 20, 4))):
                v = src[0, :, :] if len(src.shape) == 3 else src.rearrange("l (r c) -> (l r) c", c=P)
                act.dma_start(vecs[lo:lo + n, :], v).then_inc(vecs_in[i], 16)
            act.wait_ge(edge_c, 3)
            a.activation(stat[:, 15:16], epsc[:], ACT.Sqrt).then_inc(warm, 1)
            act.wait_ge(x_in[0], 16)
            a.activation(xn[:, 0, :], xres[:, 0, :], ACT.Square,
                         accum_out=stat[:, 0:1]).then_inc(ssq, 1)
            act.wait_ge(ssq, 1)
            a.activation(stat[:, 2:3], stat[:, 0:1], ACT.Sqrt, scale=1.0 / D,
                         bias=epsc[:]).then_inc(rtd, 1)
            act.wait_ge(ssq1, 1)
            a.activation(stat[:, 3:4], stat[:, 1:2], ACT.Sqrt, scale=1.0 / D,
                         bias=epsc[:]).then_inc(rtd, 1)

            act.dma_start(wpool[:], w_pool[0].rearrange("g c d -> c g d")).then_inc(wpool_in, 16)
            act.dma_start(wrouter[:], w_router[0].rearrange("(k p) e -> p k e", p=P)).then_inc(
                wrouter_in, 16)
            act.dma_start(brow[:], b_router.broadcast_to([P, NE])).then_inc(brow_in, 16)
            act.dma_start(wide[0:NE, :], b_down[0]).then_inc(bdown_in, 16)

            act.wait_ge(qk_ok, 1)
            for b in range(2):
                a.activation(qkT[:, 2 * b:2 * b + 2, :],
                             bank[b][:].rearrange("p (a t) -> p a t", a=2), ACT.Copy,
                             scale=float(HD) ** -0.5).then_inc(q_c, 1)

            def softplus_tail(j):
                t = lw[j % 2]
                act.wait_ge(z_ok, j + 1)
                if j >= 2:
                    act.wait_ge(zc_ok, j - 1)
                for h in range(2):
                    a.activation(t[:, h, :], bank[2 * (j % 2) + h][:, 0:384], ACT.Abs).then_inc(t1, 1)
                act.wait_ge(t1, 2 * j + 2)
                a.activation(t[:], t[:], ACT.Exp, scale=-1.0).then_inc(t2, 1)
                act.wait_ge(t2, j + 1)
                a.activation(t[:], t[:], ACT.Ln, bias=1.0).then_inc(t3, 1)

            def weights_exp(j):
                act.wait_ge(zc_ok, j + 1)
                if j >= 2:
                    act.wait_ge(o_ok, j - 1)
                for h in range(2):
                    a.activation(aw[j % 2][:, h, :], bank[2 * (j % 2) + h][:, 0:384],
                                 ACT.Exp).then_inc(a_exp, 1)

            def square_out(j):
                act.wait_ge(o_c, j + 1)
                if j >= 1:
                    act.wait_ge(ms_ok, j)
                a.activation(sq[:], mixT[j], ACT.Square).then_inc(sq_ok, 1)

            def pooled_out(b):
                act.wait_ge(pool_ok, b + 1)
                for g in (2 * b, 2 * b + 1):
                    a.activation(mixT[4 + g], bank[6 + b][:, (g % 2) * S:(g % 2 + 1) * S],
                                 ACT.Copy, scale=PSC[:, g:g + 1]).then_inc(poolT_ok, 1)

            softplus_tail(0)
            softplus_tail(1)
            act.wait_ge(v_ok, 1)
            a.activation(vtok[:, 0, :], bank[4][:], ACT.Copy).then_inc(v_c, 1)
            weights_exp(0)
            weights_exp(1)
            square_out(0)
            softplus_tail(2)
            square_out(1)
            softplus_tail(3)
            pooled_out(0)
            weights_exp(2)
            weights_exp(3)
            square_out(2)
            pooled_out(1)
            square_out(3)
            act.wait_ge(ms_ok, NPAIR)
            for b in range(2):
                a.activation(lw[b][:].rearrange("p a b -> p (a b)")[:, 0:HALF], bank[4 + b][:],
                             ACT.Sqrt, bias=epsc[:]).then_inc(hs_rt, 1)
            for tt in range(TT):
                act.wait_ge(x2_ok, 2 * tt + 2)
                a.activation(xn[:, tt, :], xres[:, tt, :], ACT.Square,
                             accum_out=stat[:, 4 + tt:5 + tt]).then_inc(ssq, 1)
                act.wait_ge(ssq, tt + 2)
                a.activation(stat[:, 6 + tt:7 + tt], stat[:, 4 + tt:5 + tt], ACT.Sqrt,
                             scale=1.0 / D, bias=epsc[:]).then_inc(rtd, 1)
            act.wait_ge(ntop, 1)
            for tt in range(TT):
                a.activation(ex[:, tt, :], lg[:, tt, 0:NE], ACT.Exp,
                             bias=negtop[:, tt:tt + 1]).then_inc(ex_ok, 1)

            act.wait_ge(flag_ok, 1)
            crowded = act.value_load(flag[0:1, 0:1], min_val=0, max_val=1)

            def fast_expert(e, r):
                act.wait_ge(gc_ok, e + 1)
                a.activation(sig, gatec, ACT.Sigmoid, scale=ALPHA).then_inc(sig_ok, 1)
                act.wait_ge(hT_ok, e + 1)
                a.activation(hidT, BG[:].rearrange("p (j t) -> p j t", j=4), ACT.Copy).then_inc(hT_c, 1)
                act.wait_ge(chunks_used, (e + 1) * PER_EXPERT)
                lo = (r % 2) * SLOTS
                a.activation(ypair[lo:lo + SLOTS, 0:HALF], BY[0:SLOTS, :], ACT.Copy).then_inc(y_lo, 1)

            with act.If(crowded):
                with act.Fori(0, NE) as e:
                    for tt in range(TT):
                        for hf in range(2):
                            n = e * 4 + (2 * tt + hf + 1)
                            act.wait_ge(n_gc, n)
                            a.activation(sig, gatec, ACT.Sigmoid, scale=ALPHA).then_inc(n_sig, 1)
                            act.wait_ge(n_hT, n)
                            a.activation(hidT_all[:, 4 * hf:4 * hf + 4, :],
                                         BG[:].rearrange("p (j t) -> p j t", j=4),
                                         ACT.Copy).then_inc(n_hTc, 1)
            with act.Else():
                with act.Fori(0, NE // 2) as q:
                    for r in range(2):
                        fast_expert(q * 2 + r, r)

            for tt in range(TT):
                for hf in range(2):
                    n = 2 * tt + hf
                    act.wait_ge(sum_ok, n + 1)
                    a.activation(xn[:, tt, hf * HALF:(hf + 1) * HALF],
                                 xres[:, tt, hf * HALF:(hf + 1) * HALF], ACT.Square,
                                 accum_out=stat[:, n:n + 1]).then_inc(fsq, 1)
                act.wait_ge(fadd, tt + 1)
                a.activation(stat[:, 10 + tt:11 + tt], stat[:, 8 + tt:9 + tt], ACT.Sqrt,
                             scale=1.0 / D, bias=epsc[:]).then_inc(frt, 1)

        @block.vector
        def _(dve):
            v = nc.vector
            v.memset(ones[:], 1.0).then_inc(consts, 1)
            v.memset(headmean[:], 0.0).then_inc(edge_c, 1)
            dve.wait_ge(edge_c, 1)
            for h in range(2):
                v.memset(headmean[h * HD:(h + 1) * HD, h * HD:(h + 1) * HD],
                         1.0 / HD).then_inc(consts, 1)
            v.memset(negones[:], -1.0).then_inc(edge_c, 1)
            v.memset(epsc[:], EPS).then_inc(edge_c, 1)
            v.memset(rank[:], -1.0).then_inc(edge_c, 1)
            v.memset(lg[:, :, NE:NE + 4], SENTINEL).then_inc(edge_c, 1)
            dve.wait_ge(iota_f, 1)
            for g in range(NG):
                v.tensor_scalar(edge[:, g, :], iota[:, 0:16], 1.0, float(WINDOWS[g]), ALU.add,
                                ALU.min).then_inc(edge_c, 1)
            dve.wait_ge(edge_c, 9)
            v.reciprocal(edge[:], edge[:]).then_inc(edge_c, 1)
            dve.wait_ge(edge_c, 10)
            for g in range(NG):
                v.tensor_scalar(edge[:, g, :], edge[:, g, :], float(WINDOWS[g]), None,
                                ALU.mult).then_inc(edge_c, 1)
            v.memset(gtab[:, :, :, 0:2], 0.0).then_inc(edge_c, 1)
            dve.wait_ge(x_in[1], 16)
            v.tensor_tensor_reduce(out=xn[:, 1, :], in0=xres[:, 1, :], in1=xres[:, 1, :], scale=1.0,
                                   scalar=0.0, op0=ALU.mult, op1=ALU.add,
                                   accum_out=stat[:, 1:2]).then_inc(ssq1, 1)

            def normalise(tt, nth, col):
                dve.wait_ge(rtd, nth)
                v.reciprocal(stat[:, col:col + 1], stat[:, col:col + 1]).then_inc(rinv, 1)
                dve.wait_ge(rinv, nth)
                v.tensor_scalar(xn[:, tt, :], xres[:, tt, :], stat[:, col:col + 1], None,
                                ALU.mult).then_inc(xn_ok, 1)

            def gained(nth, tt, kh, dst, gains):
                dve.wait_ge(tr, nth)
                v.tensor_tensor(
                    dst[:, 4 * kh:4 * kh + 4, tt * P:(tt + 1) * P],
                    bank[4 + 2 * tt + kh][:].rearrange("p (k t) -> p k t", k=4),
                    gains[:, 4 * kh:4 * kh + 4].unsqueeze(2).to_broadcast([P, 4, P]),
                    ALU.mult).then_inc(tr_c, 1)

            for tt in range(TT):
                normalise(tt, tt + 1, 2 + tt)
            dve.wait_ge(vec_t, 1)
            v.tensor_copy(vecT[:], bank[0][:, 0:24]).then_inc(vec_c, 1)
            dve.wait_ge(vec_c, 1)
            for tt in range(TT):
                for kh in range(2):
                    gained(2 * tt + kh + 1, tt, kh, hT, G1)

            dve.wait_ge(qk_ok, 1)
            for b in range(2):
                v.tensor_copy(qkT[:, 4 + 2 * b:6 + 2 * b, :],
                              bank[2 + b][:].rearrange("p (a t) -> p a t", a=2)).then_inc(k_c, 1)

            def frames_out(b):
                dve.wait_ge(u_ok, b + 1)
                v.tensor_copy(uT[:, 2 * b:2 * b + 2, 16:16 + S],
                              bank[6 + b][:].rearrange("p (a t) -> p a t", a=2)).then_inc(u_c, 1)

            def softplus_head(j):
                t = lw[j % 2]
                dve.wait_ge(t3, j + 1)
                for h in range(2):
                    v.scalar_tensor_tensor(out=t[:, h, :], in0=bank[2 * (j % 2) + h][:, 0:384],
                                           scalar=0.0, in1=t[:, h, :], op0=ALU.max,
                                           op1=ALU.add).then_inc(l_add, 1)
                dve.wait_ge(l_add, 2 * j + 2)
                for c in (0, 256):
                    v.tensor_tensor(t[:, :, c:c + P], t[:, :, c:c + P],
                                    before[:].unsqueeze(1).to_broadcast([P, 2, P]),
                                    ALU.mult).then_inc(l_ok, 1)

            def weights_mask(j):
                t = aw[j % 2]
                dve.wait_ge(a_exp, 2 * j + 2)
                for c in (0, 256):
                    for h in range(2):
                        v.scalar_tensor_tensor(out=t[:, h, c:c + P], in0=t[:, h, c:c + P], scalar=1.0,
                                               in1=before[:], op0=ALU.min,
                                               op1=ALU.mult).then_inc(a_ok, 1)

            def heads_out(j):
                dve.wait_ge(o_ok, j + 1)
                v.tensor_copy(mixT[j], bank[4 + j % 2][:, 0:S]).then_inc(o_c, 1)

            def pool_mix(g):
                w = win[g % 2]
                dve.wait_ge(win_add, (g + 1) * (g + 2) // 2)
                v.tensor_tensor(w[:, 16:32], w[:, 16:32], edge[:, g, :], ALU.mult).then_inc(win_out, 1)
                dve.wait_ge(win_out, g + 1)
                v.scalar_tensor_tensor(out=uT[:, g, 16:16 + S], in0=w[:, 16:16 + S],
                                       scalar=1.0 / WINDOWS[g], in1=uT[:, g, 16:16 + S],
                                       op0=ALU.mult, op1=ALU.subtract).then_inc(mix_ok, 1)

            dve.wait_ge(consts, 9)
            dve.wait_ge(edge_c, 15)
            softplus_head(0)
            softplus_head(1)
            dve.wait_ge(v_ok, 1)
            v.tensor_copy(vtok[:, 1, :], bank[5][:]).then_inc(v2_c, 1)
            weights_mask(0)
            weights_mask(1)
            frames_out(0)
            heads_out(0)
            heads_out(1)
            pool_mix(0)
            pool_mix(1)
            softplus_head(2)
            softplus_head(3)
            frames_out(1)
            weights_mask(2)
            weights_mask(3)
            pool_mix(2)
            heads_out(2)
            pool_mix(3)
            heads_out(3)
            for b in range(2):
                r = lw[b][:].rearrange("p a b -> p (a b)")[:, 0:HALF]
                dve.wait_ge(hs_rt, b + 1)
                v.reciprocal(r, r).then_inc(hs_inv, 1)
            for j in range(NPAIR):
                b, lo = j % 2, (0 if j >= 2 else S)
                r = lw[b][:].rearrange("p a b -> p (a b)")[:, lo:lo + S]
                dve.wait_ge(hs_inv, b + 1)
                v.scalar_tensor_tensor(out=mixT[j], in0=mixT[j], scalar=SBG[:, j:j + 1],
                                       in1=r, op0=ALU.mult, op1=ALU.mult).then_inc(sbn, 1)
            def residual(tt):
                dve.wait_ge(wo_ok, tt + 1)
                for hf in range(2):
                    v.tensor_tensor(xres[:, tt, hf * HALF:(hf + 1) * HALF],
                                    xres[:, tt, hf * HALF:(hf + 1) * HALF], bank[2 * tt + hf][:],
                                    ALU.add).then_inc(x2_ok, 1)

            residual(0)
            gained(5, 0, 0, h2T, G2)
            gained(6, 0, 1, h2T, G2)
            residual(1)
            normalise(0, 3, 6)
            gained(7, 1, 0, h2T, G2)
            gained(8, 1, 1, h2T, G2)
            normalise(1, 4, 7)

            dve.wait_ge(brow_in, 16)
            for tt in range(TT):
                dve.wait_ge(lg_ok, tt + 1)
                v.scalar_tensor_tensor(out=lg[:, tt, 0:NE], in0=bank[tt][:, 0:NE],
                                       scalar=stat[:, 6 + tt:7 + tt], in1=brow[:], op0=ALU.mult,
                                       op1=ALU.add).then_inc(lg_c, 1)
            dve.wait_ge(lg_c, 2)
            for tt in range(TT):
                v.max(out=top8[:, tt, :], in_=lg[:, tt, 0:NE]).then_inc(mx, 1)
            dve.wait_ge(mx, 2)
            v.tensor_scalar(negtop[:], top8[:, :, 0], -1.0, None, ALU.mult).then_inc(ntop, 1)
            v.memset(top8[:, :, TOP_K:8], SENTINEL).then_inc(t8, 1)
            dve.wait_ge(t8, 1)
            for tt in range(TT):
                v.match_replace(out=lgr[:, tt, :], in_to_replace=top8[:, tt, :],
                                in_values=lg[:, tt, :], imm_value=TAKEN).then_inc(mr, 1)
            dve.wait_ge(mr, 2)
            v.tensor_scalar(mask[:], lgr[:, :, 0:NE], TAKEN, None, ALU.is_ge).then_inc(mask_ok, 1)
            def pick_rows(q, p):
                for tt in range(TT):
                    for r in range(2):
                        d = v.tensor_scalar(pick[p][:, tt, r * SLOTS:(r + 1) * SLOTS],
                                            iota[:, 0:SLOTS], rank[:, tt, bass.ds(2 * q + r, 1)], None,
                                            ALU.is_equal)
                d.then_inc(pick_ok, 1)

            def scatter_matrix(q, p):
                dve.wait_ge(info_ok, q + 1)
                v.tensor_copy(info[:], BM[:, 0:3]).then_inc(info_c, 1)
                dve.wait_ge(info_c, q + 1)
                for r in range(2):
                    lo = r * SLOTS
                    d = v.tensor_scalar(scat[p][lo:lo + SLOTS, :], iota[lo:lo + SLOTS, :],
                                        info[lo:lo + SLOTS, 2:3], info[lo:lo + SLOTS, r:r + 1],
                                        ALU.is_equal, ALU.mult)
                d.then_inc(scat_ok, 1)

            def gathered(q, p, kh, ready, done):
                dve.wait_ge(ready, q + 1)
                v.tensor_tensor(xT[p][:, 4 * kh:4 * kh + 4, :],
                                BM[:].rearrange("p (k t) -> p k t", k=4),
                                G2[:, 4 * kh:4 * kh + 4].unsqueeze(2).to_broadcast([P, 4, P]),
                                ALU.mult).then_inc(done, 1)

            dve.wait_ge(rank_ok, 1)
            v.scalar_tensor_tensor(out=rank[:, :, 0:NE],
                                   in0=bank[2][:, 0:TT * NE].rearrange("p (a e) -> p a e", a=TT),
                                   scalar=1.0, in1=mask[:], op0=ALU.add,
                                   op1=ALU.mult).then_inc(rank_p, 1)
            v.reduce_max(most[:, 0:1], bank[2][0:1, TT * NE:(TT + 1) * NE], AX_X).then_inc(cnt_m, 1)
            dve.wait_ge(rank_p, 1)
            v.tensor_scalar(rank[:, :, 0:NE], rank[:, :, 0:NE], -1.0, None, ALU.add).then_inc(
                rank_c, 1)
            dve.wait_ge(cnt_m, 1)
            v.tensor_scalar(flag[:], most[:, 0:1], float(SLOTS), None, ALU.is_gt).then_inc(flag_ok, 1)
            dve.wait_ge(rank_c, 1)
            pick_rows(0, 0)
            dve.wait_ge(mask_ok, 1)
            dve.wait_ge(ex_ok, 2)
            v.tensor_tensor(exm[:], ex[:], mask[:], ALU.mult).then_inc(exm_ok, 1)
            dve.wait_ge(exm_ok, 1)
            v.reduce_sum(stat[:, 12:14], exm[:], AX_X).then_inc(den, 1)
            dve.wait_ge(den, 1)
            dve.wait_ge(warm, 1)
            v.reciprocal(stat[:, 14:16], stat[:, 12:14]).then_inc(den, 1)
            dve.wait_ge(den, 2)
            for tt in range(TT):
                v.tensor_scalar(gate[:, tt, :], exm[:, tt, :], stat[:, 14 + tt:15 + tt], None,
                                ALU.mult).then_inc(gate_ok, 1)
            dve.wait_ge(gate_ok, 2)
            dve.wait_ge(pool_c, 7)
            for tt in range(TT):
                v.tensor_copy(gtab[:, tt, 0:NE // 2, 0:2],
                              gate[:, tt, :].rearrange("p (q r) -> p q r", r=2)).then_inc(gtab_ok, 1)
            gathered(0, 0, 0, ga_ok, xa_ok)
            gathered(0, 0, 1, gb_ok, xb_ok)
            dve.wait_ge(gT_ok, 1)
            v.tensor_copy(gateT[:], bank[3][0:NE, 0:S]).then_inc(gT_c, 1)
            scatter_matrix(0, 0)

            dve.wait_ge(flag_ok, 1)
            crowded = dve.value_load(flag[0:1, 0:1], min_val=0, max_val=1)

            def swiglu(n, ready, gbank, ubank, gc, uc, sg, tm, hh):
                dve.wait_ge(ready[0], ready[1])
                v.tensor_scalar(gatec, gbank[:], LIMIT, None, ALU.min).then_inc(gc, 1)
                v.tensor_scalar(upc, ubank[:], LIMIT, -LIMIT, ALU.min, ALU.max).then_inc(uc, 1)
                dve.wait_ge(gc, n)
                dve.wait_ge(uc, n)
                v.scalar_tensor_tensor(out=act_t, in0=upc, scalar=1.0, in1=gatec, op0=ALU.add,
                                       op1=ALU.mult).then_inc(tm, 1)
                dve.wait_ge(tm, n)
                dve.wait_ge(sg, n)
                v.tensor_tensor(act_h, act_t, sig, ALU.mult).then_inc(hh, 1)

            def rows_out(e, r):
                dve.wait_ge(chunks_used, (e + 1) * PER_EXPERT)
                lo = (r % 2) * SLOTS
                v.tensor_copy(ypair[lo:lo + SLOTS, HALF:D], BY[SLOTS:P, :]).then_inc(y_hi, 1)

            def fast_pair(q, p):
                pick_rows(q + 1, 1 - p)
                swiglu(2 * q + 1, (chunks_used, q * (2 * PER_EXPERT) + UP_CHUNKS), BG, BU, gc_ok, uc_ok, sig_ok, t_ok, h_ok)
                scatter_matrix(q + 1, 1 - p)
                rows_out(2 * q, 0)
                swiglu(2 * q + 2, (chunks_used, q * (2 * PER_EXPERT) + (PER_EXPERT + UP_CHUNKS)), BG, BU, gc_ok, uc_ok, sig_ok, t_ok, h_ok)
                gathered(q + 1, 1 - p, 0, ga_ok, xa_ok)
                gathered(q + 1, 1 - p, 1, gb_ok, xb_ok)
                rows_out(2 * q + 1, 1)

            with dve.If(crowded):
                for tt in range(TT):
                    for kh in range(2):
                        gained(9 + 2 * tt + kh, tt, kh, h2T, G2)
                dve.wait_ge(bd_ok, 1)
                for tt in range(TT):
                    for hf in range(2):
                        v.tensor_copy(xn[:, tt, hf * HALF:(hf + 1) * HALF],
                                      bank[2 * tt + hf][:]).then_inc(n_acc, 1)
                with dve.Fori(0, NE) as e:
                    for tt in range(TT):
                        for hf in range(2):
                            swiglu(e * 4 + (2 * tt + hf + 1), (n_up, e * 2 + (tt + 1)), bank[hf],
                                   bank[2 + hf], n_gc, n_uc, n_sig, n_t, n_h)
                        if tt == 0:
                            dve.wait_ge(n_y, e + 1)
                        else:
                            dve.wait_ge(chunks_used, (e + 1) * PER_EXPERT)
                        dve.wait_ge(n_acc, e * 4 + (2 * tt + 4))
                        for hf in range(2):
                            v.scalar_tensor_tensor(
                                out=xn[:, tt, hf * HALF:(hf + 1) * HALF], in0=bank[5 + hf][:],
                                scalar=gate[:, tt, bass.ds(e, 1)],
                                in1=xn[:, tt, hf * HALF:(hf + 1) * HALF], op0=ALU.mult,
                                op1=ALU.add).then_inc(n_acc, 1)
                dve.wait_ge(n_acc, 4 * NE + 4)
                for tt in range(TT):
                    for hf in range(2):
                        v.tensor_tensor(xres[:, tt, hf * HALF:(hf + 1) * HALF],
                                        xres[:, tt, hf * HALF:(hf + 1) * HALF],
                                        xn[:, tt, hf * HALF:(hf + 1) * HALF],
                                        ALU.add).then_inc(sum_ok, 1)
            with dve.Else():
                with dve.Fori(0, NE // BODY) as i:
                    for p in range(2):
                        fast_pair(i * 2 + p, p)
                for tt in range(TT):
                    for hf in range(2):
                        dve.wait_ge(last_ok, 2 * tt + hf + 1)
                        v.tensor_tensor(xres[:, tt, hf * HALF:(hf + 1) * HALF],
                                        xres[:, tt, hf * HALF:(hf + 1) * HALF],
                                        bank[2 * tt + hf][:], ALU.add).then_inc(sum_ok, 1)

            dve.wait_ge(fg_in, 16)
            for tt in range(TT):
                dve.wait_ge(fsq, 2 * tt + 2)
                v.tensor_tensor(stat[:, 8 + tt:9 + tt], stat[:, 2 * tt:2 * tt + 1],
                                stat[:, 2 * tt + 1:2 * tt + 2], ALU.add).then_inc(fadd, 1)
            for tt in range(TT):
                dve.wait_ge(frt, tt + 1)
                v.reciprocal(stat[:, 10 + tt:11 + tt], stat[:, 10 + tt:11 + tt]).then_inc(finv, 1)
                dve.wait_ge(finv, tt + 1)
                for hf in range(2):
                    v.scalar_tensor_tensor(out=xn[:, tt, hf * HALF:(hf + 1) * HALF],
                                           in0=xres[:, tt, hf * HALF:(hf + 1) * HALF],
                                           scalar=stat[:, 10 + tt:11 + tt],
                                           in1=wide[:, hf * HALF:(hf + 1) * HALF], op0=ALU.mult,
                                           op1=ALU.mult).then_inc(fin, 1)

        @block.tensor
        def _(pe):
            t = nc.tensor

            def mm(o, l, r, start=False, stop=False):
                return t.matmul(o, l, r, start=start, stop=stop, skip_group_check=True)

            for i in range(4):
                pe.wait_ge(vecs_in[i], 16)
            pe.wait_ge(consts, 9)
            t.transpose(bank[0][:, 0:24], vecs[:], ident[0:24, 0:24]).then_inc(vec_t, 1)

            def turn(src, tt):
                for kh in range(2):
                    for k in range(4):
                        lo = (4 * kh + k) * P
                        m = t.transpose(bank[4 + 2 * tt + kh][:, k * P:(k + 1) * P],
                                        src[:, tt, lo:lo + P], ident[:])
                    m.then_inc(tr, 1)

            for tt in range(TT):
                pe.wait_ge(xn_ok, tt + 1)
                turn(xn, tt)
            pe.wait_ge(tr_c, 3)
            for k in range(KD):
                if k == 4:
                    pe.wait_ge(tr_c, 4)
                pe.wait_ge(wqk_in[k], 16)
                for c in range(8):
                    m = mm(bank[c // 2][:, (c % 2) * S:(c % 2 + 1) * S],
                           w_qk[:, k, c * P:(c + 1) * P], hT[:, k, :],
                           start=(k == 0 and c % 2 == 0), stop=(k == KD - 1 and c % 2 == 1))
            m.then_inc(qk_ok, 1)

            def project_v():
                for k in range(KD):
                    if k % 4 == 0:
                        pe.wait_ge(wv_in[k // 4], 16)
                    for tt in range(TT):
                        m = mm(bank[4 + tt][:], hT[:, k, tt * P:(tt + 1) * P], w_v[:, k, :],
                               start=(k == 0), stop=(k == KD - 1))
                m.then_inc(v_ok, 1)

            def project_u(b):
                for k in range(KD):
                    if b == 0 and k % 4 == 0:
                        pe.wait_ge(wu_in[k // 4], 16)
                    for c in (2 * b, 2 * b + 1):
                        m = mm(bank[6 + b][:, (c % 2) * S:(c % 2 + 1) * S],
                               w_u[:, k, c * P:(c + 1) * P], hT[:, k, :],
                               start=(k == 0 and c % 2 == 0), stop=(k == KD - 1 and c % 2 == 1))
                m.then_inc(u_ok, 1)

            pe.wait_ge(q_c, 2)
            pe.wait_ge(k_c, 2)

            def scores(j):
                if j >= 2:
                    pe.wait_ge(a_exp, 2 * j - 2)
                for h in range(2):
                    zb = bank[2 * (j % 2) + h]
                    q = qkT[h * HD:(h + 1) * HD, j, :]
                    kk = qkT[h * HD:(h + 1) * HD, NPAIR + j, :]
                    mm(zb[:, 0:S], kk[:, 0:P], q, start=True)
                    m = mm(zb[:, S:S + P], kk[:, P:S], q[:, P:S])
                m.then_inc(z_ok, 1)

            def after_sums(j):
                pe.wait_ge(l_ok, 2 * j + 2)
                for h in range(2):
                    zb = bank[2 * (j % 2) + h]
                    lt = lw[j % 2][:, h, :]
                    mm(zb[:, 0:S], negtri[:], lt[:, 0:S])
                    mm(zb[:, P:S], negones[:], lt[:, S:S + P])
                    m = mm(zb[:, S:S + P], negtri[:], lt[:, S:S + P], stop=True)
                m.then_inc(zc_ok, 1)

            def values(j):
                pe.wait_ge(a_ok, 4 * j + 4)
                if j >= 2:
                    pe.wait_ge(o_c, j - 1)
                for h in range(2):
                    hd = (2 * j + h) * HD
                    ob = bank[4 + j % 2][h * HD:(h + 1) * HD, :]
                    wt = aw[j % 2][:, h, :]
                    mm(ob[:, 0:S], vtok[:, 0, hd:hd + HD], wt[:, 0:S], start=True)
                    m = mm(ob[:, P:S], vtok[:, 1, hd:hd + HD], wt[:, S:S + P], stop=True)
                m.then_inc(o_ok, 1)

            def mean_squares(j):
                pe.wait_ge(sq_ok, j + 1)
                lo = 0 if j >= 2 else S
                mm(bank[4 + j % 2][:, lo:lo + S], headmean[:], sq[:], start=True,
                   stop=True).then_inc(ms_ok, 1)

            def map_pooled(b):
                if b == 0:
                    pe.wait_ge(wpool_in, 16)
                for g in (2 * b, 2 * b + 1):
                    pe.wait_ge(mix_ok, g + 1)
                    m = mm(bank[6 + b][:, (g % 2) * S:(g % 2 + 1) * S], wpool[:, g, :],
                           uT[:, g, 16:16 + S], start=(g % 2 == 0), stop=(g % 2 == 1))
                m.then_inc(pool_ok, 1)

            def output(tt, n):
                k = WO_ROWS[n // 2] + n % 2
                if n % 2 == 0:
                    pe.wait_ge(wout_in[n // 2], 16)
                if k >= 4:
                    pe.wait_ge(poolT_ok, k - 3)
                else:
                    pe.wait_ge(sbn, k + 1)
                for hf in range(2):
                    m = mm(bank[2 * tt + hf][:], mixT[k][:, tt * P:(tt + 1) * P],
                           w_o[:, n, hf * HALF:(hf + 1) * HALF], start=(n == 0),
                           stop=(n == KD - 1))
                return m

            pe.wait_ge(edge_c, 15)
            scores(0)
            scores(1)
            project_v()
            after_sums(0)
            after_sums(1)
            project_u(0)
            pe.wait_ge(v_c, 1)
            pe.wait_ge(v2_c, 1)
            values(0)
            values(1)
            scores(2)
            scores(3)
            mean_squares(0)
            project_u(1)
            mean_squares(1)
            map_pooled(0)
            after_sums(2)
            after_sums(3)
            values(2)
            output(0, 0)
            output(0, 1)
            values(3)
            map_pooled(1)
            mean_squares(2)
            output(0, 2)
            output(0, 3)
            mean_squares(3)
            for n in range(4):
                m = output(1, n)
            m.then_inc(wo_half, 1)
            for n in range(4, KD):
                m = output(0, n)
            m.then_inc(wo_ok, 1)
            output(1, 4)
            output(1, 5)

            def logits(tt):
                pe.wait_ge(tr_c, 4 + 2 * tt + 2)
                for k in range(KD):
                    m = mm(bank[tt][:, 0:NE], h2T[:, k, tt * P:(tt + 1) * P], wrouter[:, k, :],
                           start=(k == 0), stop=(k == KD - 1))
                m.then_inc(lg_ok, 1)

            pe.wait_ge(x2_ok, 2)
            turn(xres, 0)
            output(1, 6)
            output(1, 7).then_inc(wo_ok, 1)
            pe.wait_ge(wrouter_in, 16)
            logits(0)
            pe.wait_ge(x2_ok, 4)
            turn(xres, 1)
            logits(1)
            pe.wait_ge(mask_ok, 1)
            mm(bank[2][:, 0:NE], before[:], mask[:, 0, :], start=True)
            mm(bank[2][:, NE:2 * NE], before[:], mask[:, 1, :])
            mm(bank[2][:, NE:2 * NE], ones[:], mask[:, 0, :])
            mm(bank[2][:, 2 * NE:3 * NE], ones[:], mask[:, 0, :])
            mm(bank[2][:, 2 * NE:3 * NE], ones[:], mask[:, 1, :], stop=True).then_inc(rank_ok, 1)
            def slot_info(q, p):
                for tt in range(TT):
                    m = mm(BM[:, 0:3], pick[p][:, tt, :], gtab[:, tt, bass.ds(q, 1), :].rearrange(
                        "p a b -> p (a b)"), start=(tt == 0), stop=(tt == 1))
                m.then_inc(info_ok, 1)

            def gather(q, p, kh, free, done):
                if free is not None:
                    pe.wait_ge(free, q + 1)
                for k in range(4):
                    f = (4 * kh + k) * P
                    for tt in range(TT):
                        m = mm(BM[:, k * P:(k + 1) * P], xn[:, tt, f:f + P], pick[p][:, tt, :],
                               start=(k == 0 and tt == 0), stop=(k == 3 and tt == 1))
                m.then_inc(done, 1)

            pe.wait_ge(pick_ok, 1)
            pe.wait_ge(xn_ok, 4)
            gather(0, 0, 0, None, ga_ok)
            gather(0, 0, 1, xa_ok, gb_ok)
            pe.wait_ge(gate_ok, 2)
            for tt in range(TT):
                m = t.transpose(bank[3][0:NE, tt * P:(tt + 1) * P], gate[:, tt, :], ident[:])
            m.then_inc(gT_ok, 1)
            pe.wait_ge(xb_ok, 1)
            pe.wait_ge(gtab_ok, 2)
            slot_info(0, 0)

            def add_b_down():
                pe.wait_ge(bdown_in, 16)
                pe.wait_ge(gT_c, 1)
                for tt in range(TT):
                    for hf in range(2):
                        m = mm(bank[2 * tt + hf][:], gateT[:, tt * P:(tt + 1) * P],
                               wide[0:NE, hf * HALF:(hf + 1) * HALF], start=True)
                m.then_inc(bd_ok, 1)

            pe.wait_ge(flag_ok, 1)
            crowded = pe.value_load(flag[0:1, 0:1], min_val=0, max_val=1)

            def chunk_wait(i, m):
                pe.wait_ge(chunk_in[slot_of(m)], i * (16 * GEN) + 16 * (m // RING + 1))

            def combine(q, p):
                pe.wait_ge(scat_ok, q + 1)
                pe.wait_ge(y_lo, 2 * q + 2)
                pe.wait_ge(y_hi, 2 * q + 2)
                for tt in range(TT):
                    for hf in range(2):
                        m = mm(bank[2 * tt + hf][:], scat[p][:, tt * P:(tt + 1) * P],
                               ypair[:, hf * HALF:(hf + 1) * HALF])
                m.then_inc(comb_ok, 1)

            def fast_expert(i, r, q, p, not_first):
                e = 2 * q + r % 2
                m0 = r * PER_EXPERT
                cols = slice((r % 2) * SLOTS, (r % 2 + 1) * SLOTS)
                pe.wait_ge(bias_in[r % 2], i * 32 + 16 * (r // 2 + 1))
                mm(BG[:], bsel[:, 0, :], bias[:, r % 2, :], start=True)
                mm(BU[:], bsel[:, 1, :], bias[:, r % 2, :], start=True).then_inc(bias_used, 1)
                if r % 2 == 0:
                    pe.wait_ge(xb_ok, q + 1)
                for k in range(KD):
                    chunk_wait(i, m0 + k)
                    for gu, b in ((0, BG), (1, BU)):
                        for hf in range(2):
                            m = mm(b[hf * SLOTS:(hf + 1) * SLOTS, :], xT[p][:, k, cols],
                                   up_w(m0 + k, gu, hf), stop=(k == KD - 1))
                    m.then_inc(chunks_used, 1)
                if r % 2 == 0:
                    if not_first:
                        combine(q - 1, 1 - p)
                    else:
                        add_b_down()
                else:
                    gather(q + 1, 1 - p, 0, info_c, ga_ok)
                pe.wait_ge(h_ok, e + 1)
                for j in range(4):
                    m = t.transpose(BG[:, j * P:(j + 1) * P], act_h[:, j * P:(j + 1) * P], ident[:])
                m.then_inc(hT_ok, 1)
                if r % 2 == 0:
                    pe.wait_ge(pick_ok, q + 2)
                    slot_info(q + 1, 1 - p)
                else:
                    gather(q + 1, 1 - p, 1, xa_ok, gb_ok)
                pe.wait_ge(hT_c, e + 1)
                for c in range(DOWN_CHUNKS):
                    n = m0 + UP_CHUNKS + c
                    chunk_wait(i, n)
                    for s in range(2):
                        f = 2 * c + s
                        half, j = f // 4, f % 4
                        for hf in range(2):
                            m = mm(BY[hf * SLOTS:(hf + 1) * SLOTS, :],
                                   hidT[:, j, half * SLOTS:(half + 1) * SLOTS], down_w(n, s, hf),
                                   start=(f == 0), stop=(f == KF - 1))
                    m.then_inc(chunks_used, 1)

            def fast_body(i, first):
                for r in range(BODY):
                    q = i * 2 + r // 2
                    fast_expert(i, r, q, r // 2, not (first and r < 2))

            with pe.If(crowded):
                add_b_down()
                pe.wait_ge(info_c, 1)
                for tt in range(TT):
                    turn(xn, tt)
                pe.wait_ge(n_acc, 4)
                pe.wait_ge(tr_c, 12)

                def all_tokens(i, r):
                    e = i * BODY + r
                    m0 = r * PER_EXPERT
                    pe.wait_ge(bias_in[r % 2], i * 32 + 16 * (r // 2 + 1))
                    for tt in range(TT):
                        for b in range(4):
                            m = mm(bank[b][:], bsel[:, 2 + b, :], bias[:, r % 2, :], start=True)
                        if tt == TT - 1:
                            m.then_inc(bias_used, 1)
                        for k in range(KD):
                            if tt == 0:
                                chunk_wait(i, m0 + k)
                            for b in range(4):
                                m = mm(bank[b][:], h2T[:, k, tt * P:(tt + 1) * P],
                                       up_w(m0 + k, b // 2, b % 2), stop=(k == KD - 1))
                        m.then_inc(n_up, 1)
                        for hf in range(2):
                            n = e * 4 + (2 * tt + hf + 1)
                            pe.wait_ge(n_h, n)
                            if hf == 1:
                                pe.wait_ge(n_hTc, e * 4 + (2 * tt + 1))
                            for j in range(4):
                                m = t.transpose(BG[:, j * P:(j + 1) * P],
                                                act_h[:, j * P:(j + 1) * P], ident[:])
                            m.then_inc(n_hT, 1)
                        pe.wait_ge(n_hTc, e * 4 + (2 * tt + 2))
                        pe.wait_ge(n_acc, e * 4 + (2 * tt + 4))
                        for f in range(KF):
                            n = m0 + UP_CHUNKS + f // 2
                            if tt == 0 and f % 2 == 0:
                                chunk_wait(i, n)
                            for hf in range(2):
                                m = mm(bank[5 + hf][:], hidT_all[:, f, :], down_w(n, f % 2, hf),
                                       start=(f == 0), stop=(f == KF - 1))
                        if tt == 0:
                            m.then_inc(n_y, 1)
                        else:
                            m.then_inc(chunks_used, PER_EXPERT)

                with pe.Fori(0, NBODY) as i:
                    for r in range(BODY):
                        all_tokens(i, r)
            with pe.Else():
                fast_body(0, True)
                with pe.Fori(1, NBODY) as i:
                    fast_body(i, False)
                pe.wait_ge(scat_ok, NE // 2)
                pe.wait_ge(y_lo, NE)
                pe.wait_ge(y_hi, NE)
                for tt in range(TT):
                    for hf in range(2):
                        mm(bank[2 * tt + hf][:], scat[1][:, tt * P:(tt + 1) * P],
                           ypair[:, hf * HALF:(hf + 1) * HALF], stop=True).then_inc(last_ok, 1)


_INS = ["x", "norm1_g", "w_in", "sb_norm_g", "w_pool", "pool_scale", "w_out", "norm2_g", "w_router",
        "b_router", "w_gate_up", "b_gate_up", "w_down", "b_down", "final_norm_g"]


def kernel(**inputs):
    import numpy as _np
    import concourse.bacc as _bacc
    from concourse import mybir as _mybir
    from concourse.bass_utils import run_bass_kernel_spmd as _run

    nc = _bacc.Bacc("TRN2", target_bir_lowering=False, num_devices=1)
    arrays, args = {}, []
    for name in _INS:
        a = _np.ascontiguousarray(inputs[name])
        arrays[f"in_{name}_dram"] = a
        args.append(nc.dram_tensor(f"in_{name}_dram", a.shape, _mybir.dt.from_np(a.dtype),
                                   kind="ExternalInput").ap())
    shape = tuple(inputs["x"].shape)
    args.append(nc.dram_tensor("out_0_dram", shape, _mybir.dt.float32, kind="ExternalOutput").ap())
    build(nc, *args)
    r = _run(nc, [arrays], core_ids=[0])
    return r.results[0]["out_0_dram"]
```

```python
from contextlib import ExitStack

import concourse.bass as bass
from concourse import mybir

F32 = mybir.dt.float32
I32 = mybir.dt.int32
BF16 = mybir.dt.bfloat16
ALU = mybir.AluOpType
ACT = mybir.ActivationFunctionType
AX_X = mybir.AxisListType.X

P = 128
EPS = 1e-5
TOP_K = 4
WINDOWS = (2, 4, 8, 16)
LIMIT = 7.0
ALPHA = 1.702
SLOTS = 64
SENTINEL = 2.0e38
TAKEN = 3.0e38


def build(nc, x, norm1_g, w_in, sb_norm_g, w_pool, pool_scale, w_out, norm2_g, w_router, b_router,
          w_gate_up, b_gate_up, w_down, b_down, final_norm_g, out):
    _, S, D = x.shape
    NIN = w_in.shape[2]
    _, NE, _, F2 = w_gate_up.shape
    F = F2 // 2
    SBW = sb_norm_g.shape[1]
    _, NG, GC, _ = w_pool.shape
    HD = 64
    TT = S // P
    KD = D // P
    KF = F // P
    NPAIR = SBW // P
    HALF = 512
    assert (S, D, F, NIN, NE, SBW, NG, GC) == (256, 1024, 1024, 2048, 32, 512, 4, 128)

    CHUNK = 2048
    RING = 16
    UP_CHUNKS = KD
    DOWN_CHUNKS = KF // 2
    PER_EXPERT = UP_CHUNKS + DOWN_CHUNKS
    BODY = 4
    NBODY = NE // BODY
    PER_BODY = BODY * PER_EXPERT
    EXTRA = 3
    PLACES = RING + EXTRA
    ORDER = [*range(12, 16), *range(0, 8), *range(RING, PLACES), *range(8, 12)]
    FIRST_PLACES = [ORDER[n % PLACES] for n in range(PER_BODY)]
    NEXT_SLOT = next(p for p in ORDER[PER_BODY % PLACES:] if p < RING)
    assert PER_BODY % RING == 0 and UP_CHUNKS == 8 and DOWN_CHUNKS == 4

    def slot_of(n, first=False):
        return FIRST_PLACES[n] if first else (NEXT_SLOT + n) % RING

    def loads_of(n, first):
        if first:
            return n // PLACES + 1
        return FIRST_PLACES.count(slot_of(n)) + n // RING + 1

    rows = {
        "wgu": w_gate_up.rearrange("l e d f -> (l e d) f"),
        "wd": w_down.rearrange("l e f d -> (l e f) d"),
        "bgu": b_gate_up.rearrange("l e (r c) -> (l e r) c", c=HALF),
    }

    with ExitStack() as ctx:
        def sb(name, shape, dt=F32):
            return ctx.enter_context(nc.sbuf_tensor(name, shape, dt))

        def sem(name):
            return ctx.enter_context(nc.semaphore(name))

        ring = sb("ring", [P, RING * CHUNK])
        w_qk = ring[:, 0:4 * CHUNK].rearrange("p (k n) -> p k n", k=KD)
        w_v = ring[:, 4 * CHUNK:6 * CHUNK].rearrange("p (k n) -> p k n", k=KD)
        w_u = ring[:, 6 * CHUNK:8 * CHUNK].rearrange("p (k n) -> p k n", k=KD)
        w_o = ring[:, 8 * CHUNK:12 * CHUNK].rearrange("p (k n) -> p k n", k=KD)
        WO_ROWS = (4, 6, 0, 2)
        xres = sb("xres", [P, TT, D])
        xn = sb("xn", [P, TT, D])
        area = sb("area", [P, 10240])

        def part(lo, n, a=None):
            v = area[:, lo:lo + n]
            return v if a is None else v.rearrange("p (a b) -> p a b", a=a)

        hT = part(0, KD * S, KD)
        mixT = [xn[:, 1, S * j:S * (j + 1)] for j in range(4)] + [part(S * j, S) for j in range(4)]
        qkT = part(2048, 2048, 8)
        vtok = part(4096, TT * SBW, TT)
        uT = part(5120, NG * (S + 16), NG)
        lw = [part(6208 + 768 * i, 768, 2) for i in range(2)]
        aw = [part(7744 + 768 * i, 768, 2) for i in range(2)]
        win = [part(9280 + 272 * i, 272) for i in range(2)]
        sq = part(9824, S)
        h2T = part(0, KD * S, KD)
        xT = [part(1024 * i, 1024, KD) for i in range(2)]
        extra = [part(2048 * (i + 1), CHUNK) for i in range(EXTRA)]
        gatec, upc, sig = [part(8192 + HALF * i, HALF) for i in range(3)]
        hidT = part(9728, HALF, 4)
        gain_f = extra[0][:, 0:D]

        wide = sb("wide", [P, D])
        ypair = wide[:]
        hidT_all = wide[:].rearrange("p (a b) -> p a b", a=KF)
        wpool = sb("wpool", [P, NG, GC])
        wrouter = sb("wrouter", [P, KD, NE])
        brow = sb("brow", [P, NE])
        bias = sb("bias", [4, 2, HALF])
        bsel = sb("bsel", [4, 6, P])
        vecs = sb("vecs", [24, P])
        vecT = sb("vecT", [P, 24])
        ident = sb("ident", [P, P])
        masks = sb("masks", [P, 4 * P])
        negtri, negones, before, headmean = [masks[:, P * i:P * (i + 1)] for i in range(4)]
        pick = [masks[:, 2 * P * i:2 * P * (i + 1)].rearrange("p (a b) -> p a b", a=TT)
                for i in range(2)]
        ones = sb("ones", [P, P], BF16)
        before_b = sb("before_b", [P, P], BF16)
        mask_b = sb("mask_b", [P, TT, NE], BF16)
        scat = [sb("scat0", [P, S])[:], wrouter[:].rearrange("p k e -> p (k e)")]
        iota = sb("iota", [P, S])
        edge = sb("edge", [P, NG, 16])
        lg = sb("lg", [P, TT, NE + 4])
        lgr = sb("lgr", [P, TT, NE + 4])
        top8 = sb("top8", [P, TT, 8])
        negtop = sb("negtop", [P, TT])
        mask = sb("mask", [P, TT, NE])
        ex = sb("ex", [P, TT, NE])
        exm = sb("exm", [P, TT, NE])
        gate = sb("gate", [P, TT, NE])
        gateT = sb("gateT", [NE, S])
        rank = sb("rank", [P, TT, NE + 2])
        gtab = sb("gtab", [P, TT, NE // 2 + 1, 3])
        info = sb("info", [P, 3])
        stat = sb("stat", [P, 16])
        epsc = sb("epsc", [P, 1])
        most = sb("most", [1, 2])
        flag = sb("flag", [1, 1], I32)
        bank = [ctx.enter_context(nc.psum_tensor(f"bank{i}", [P, HALF], F32)) for i in range(8)]
        G1, G2, SBG, PSC = vecT[:, 0:8], vecT[:, 8:16], vecT[:, 16:20], vecT[:, 20:24]
        BG, BU, BY, BM = bank[4], bank[5], bank[6], bank[7]

        x_in = [sem(f"x_in{i}") for i in range(TT)]
        vecs_in = [sem(f"vecs_in{i}") for i in range(4)]
        wpool_in, wrouter_in, brow_in, bdown_in, fg_in = map(
            sem, ("wpool_in", "wrouter_in", "brow_in", "bdown_in", "fg_in"))
        wqk_in = [sem(f"wqk_in{i}") for i in range(8)]
        wv_in = [sem(f"wv_in{i}") for i in range(2)]
        wu_in = [sem(f"wu_in{i}") for i in range(2)]
        wout_in = [sem(f"wout_in{i}") for i in range(4)]
        chunk_in = [sem(f"chunk_in{i}") for i in range(PLACES)]
        bias_in = [sem(f"bias_in{i}") for i in range(2)]
        chunks_used = sem("chunks_used")
        bias_used = sem("bias_used")
        out_done = sem("out_done")

        consts, ones_c, pool_c, iota_f, edge_c = map(sem, ("consts", "ones_c", "pool_c", "iota_f", "edge_c"))
        vec_t, vec_c = sem("vec_t"), sem("vec_c")
        warm = sem("warm")
        ssq, rtd, rinv, xn_ok = map(sem, ("ssq", "rtd", "rinv", "xn_ok"))
        tr, tr_c, tr_a, wrouter_c = map(sem, ("tr", "tr_c", "tr_a", "wrouter_c"))
        qk_ok, v_ok, u_ok, wo_half = map(sem, ("qk_ok", "v_ok", "u_ok", "wo_half"))
        q_c, k_c, v_c, v2_c, u_c = map(sem, ("q_c", "k_c", "v_c", "v2_c", "u_c"))
        win_add, win_out, mix_ok = map(sem, ("win_add", "win_out", "mix_ok"))
        z_ok, t1, t2, t3, l_add, l_ok, zc_ok, a_exp, a_ok, o_ok, o_c, sq_ok, ms_ok = map(
            sem, ("z_ok", "t1", "t2", "t3", "l_add", "l_ok", "zc_ok", "a_exp", "a_ok", "o_ok", "o_c",
                  "sq_ok", "ms_ok"))
        hs_rt, hs_inv, sbn = map(sem, ("hs_rt", "hs_inv", "sbn"))
        pool_ok, poolT_ok = sem("pool_ok"), sem("poolT_ok")
        wo_ok, x2_ok = sem("wo_ok"), sem("x2_ok")
        lg_ok, lg_c, mx, ntop, t8, mr, mask_ok, ex_ok, exm_ok, den, gate_ok = map(
            sem, ("lg_ok", "lg_c", "mx", "ntop", "t8", "mr", "mask_ok", "ex_ok", "exm_ok", "den",
                  "gate_ok"))
        maskb_ok, rank_ok, rank_c, cnt_m, flag_ok, gtab_ok, gT_ok, gT_c, bd_ok = map(
            sem, ("maskb_ok", "rank_ok", "rank_c", "cnt_m", "flag_ok", "gtab_ok", "gT_ok", "gT_c",
                  "bd_ok"))
        pick_ok, info_ok, info_c, scat_ok, ga_ok, gb_ok, xa_ok, xb_ok = map(
            sem, ("pick_ok", "info_ok", "info_c", "scat_ok", "ga_ok", "gb_ok", "xa_ok", "xb_ok"))
        gc_ok, uc_ok, sig_ok, t_ok, h_ok, hT_ok, hT_c, y_lo, y_hi, comb_ok = map(
            sem, ("gc_ok", "uc_ok", "sig_ok", "t_ok", "h_ok", "hT_ok", "hT_c",
                  "y_lo", "y_hi", "comb_ok"))
        n_up, n_gc, n_uc, n_sig, n_t, n_h, n_hT, n_hTc, n_y, n_acc = map(
            sem, ("n_up", "n_gc", "n_uc", "n_sig", "n_t", "n_h", "n_hT", "n_hTc", "n_y",
                  "n_acc"))
        last_ok, sum_ok, fsq, fadd, frt, finv, fin = map(
            sem, ("last_ok", "sum_ok", "fsq", "fadd", "frt", "finv", "fin"))

        def place(slot):
            if slot >= RING:
                return extra[slot - RING]
            return ring[:, slot * CHUNK:(slot + 1) * CHUNK]

        def up_w(slot, gu, half):
            lo = gu * F + half * HALF
            return place(slot)[:, lo:lo + HALF]

        def down_w(slot, s, half):
            lo = s * D + half * HALF
            return place(slot)[:, lo:lo + HALF]

        def head_rms(j):
            return xn[:, 0, S * j:S * (j + 1)]

        block = ctx.enter_context(nc.Block())

        @block.sync
        def _(sp):
            for tt in range(TT):
                sp.dma_start(xres[:, tt, :], x[0, tt * P:(tt + 1) * P, :]).then_inc(x_in[tt], 16)
            for k in range(KD):
                sp.dma_start(w_qk[:, k, :], w_in[0, k * P:(k + 1) * P, 0:2 * SBW]).then_inc(
                    wqk_in[k], 16)
            for w, col, done in ((w_v, 2 * SBW, wv_in), (w_u, 3 * SBW, wu_in)):
                for c in range(2):
                    sp.dma_start(w[:, 4 * c:4 * c + 4, :],
                                 w_in[0, c * HALF:(c + 1) * HALF, col:col + SBW].rearrange(
                                     "(k p) n -> p k n", p=P)).then_inc(done[c], 16)
            for c in range(4):
                row = WO_ROWS[c] * P
                sp.dma_start(w_o[:, 2 * c:2 * c + 2, :],
                             w_out[0, row:row + 2 * P, :].rearrange("(s p) n -> p s n", s=2)
                             ).then_inc(wout_in[c], 16)

            def load_expert(e, m0, first):
                r = m0 // PER_EXPERT
                if not first or r >= 2:
                    sp.wait_ge(bias_used, e - 1)
                sp.dma_start(bias[:, r % 2, :], rows["bgu"][bass.ds(e * 4, 4), :]).then_inc(
                    bias_in[r % 2], 16)
                for c in range(PER_EXPERT):
                    m = m0 + c
                    s = slot_of(m, first)
                    n = e * PER_EXPERT + c
                    if first and m < PLACES:
                        if 0 <= s < 4:
                            sp.wait_ge(qk_ok, 1)
                        elif 4 <= s < 6:
                            sp.wait_ge(v_ok, 1)
                        elif 6 <= s < 8:
                            sp.wait_ge(u_ok, 2)
                        elif s == RING:
                            sp.wait_ge(z_ok, NPAIR)
                        elif s > RING:
                            sp.wait_ge(o_ok, NPAIR)
                            sp.wait_ge(pool_ok, 2)
                        elif 8 <= s < 10:
                            sp.wait_ge(wo_half, 1)
                        elif 10 <= s < 12:
                            sp.wait_ge(wo_ok, 3)
                    elif first:
                        sp.wait_ge(chunks_used, n - (PLACES - 1))
                    else:
                        sp.wait_ge(chunks_used, n - (RING - 1))
                    dst = place(s)
                    if c < UP_CHUNKS:
                        src = rows["wgu"][bass.ds(e * D + c * P, P), :]
                    else:
                        src = rows["wd"][bass.ds(e * F + (c - UP_CHUNKS) * 2 * P, 2 * P), :].rearrange(
                            "(s p) n -> p s n", s=2)
                        dst = dst.rearrange("p (s n) -> p s n", s=2)
                    sp.dma_start(dst, src).then_inc(chunk_in[s], 16)

            for r in range(BODY):
                load_expert(r, r * PER_EXPERT, True)
            with sp.Fori(1, NBODY) as i:
                for r in range(BODY):
                    load_expert(i * BODY + r, r * PER_EXPERT, False)
            for n in range(4):
                tt, c = n // 2, (n % 2) * HALF
                sp.wait_ge(fin, n + 1)
                sp.dma_start(out[0, tt * P:(tt + 1) * P, c:c + HALF],
                             xn[:, tt, c:c + HALF]).then_inc(out_done, 16)
            sp.wait_ge(out_done, 64)

        @block.gpsimd
        def _(pool):
            g = nc.gpsimd
            g.memset(ident[:], 0.0).then_inc(pool_c, 1)
            g.memset(negtri[:], -1.0).then_inc(pool_c, 1)
            g.memset(before[:], 1.0).then_inc(pool_c, 1)
            g.memset(bsel[:], 0.0).then_inc(pool_c, 1)
            pool.wait_ge(pool_c, 4)
            g.affine_select(ident[:], ident[:], compare_op=ALU.not_equal, fill=1.0, base=0,
                            pattern=[[-1, P]], channel_multiplier=1).then_inc(consts, 1)
            g.affine_select(negtri[:], negtri[:], compare_op=ALU.is_ge, fill=0.0, base=0,
                            pattern=[[-1, P]], channel_multiplier=1).then_inc(consts, 1)
            g.affine_select(before[:], before[:], compare_op=ALU.is_gt, fill=0.0, base=0,
                            pattern=[[1, P]], channel_multiplier=-1).then_inc(consts, 1)
            g.affine_select(bsel[:, 0:2, 0:SLOTS], bsel[:, 0:2, 0:SLOTS], compare_op=ALU.not_equal,
                            fill=1.0, base=0, pattern=[[-2, 2], [0, SLOTS]],
                            channel_multiplier=1).then_inc(consts, 1)
            g.affine_select(bsel[:, 0:2, SLOTS:P], bsel[:, 0:2, SLOTS:P], compare_op=ALU.not_equal,
                            fill=1.0, base=-1, pattern=[[-2, 2], [0, SLOTS]],
                            channel_multiplier=1).then_inc(consts, 1)
            g.affine_select(bsel[:, 2:6, :], bsel[:, 2:6, :], compare_op=ALU.not_equal,
                            fill=1.0, base=0, pattern=[[-1, 4], [0, P]],
                            channel_multiplier=1).then_inc(consts, 1)
            g.iota(iota[:], pattern=[[1, S]], base=0, channel_multiplier=0,
                   allow_small_or_imprecise_dtypes=True).then_inc(iota_f, 1)
            for tt in range(TT):
                g.iota(gtab[:, tt, :, 2], pattern=[[0, NE // 2 + 1]], base=tt * P,
                       channel_multiplier=1,
                       allow_small_or_imprecise_dtypes=True).then_inc(pool_c, 1)
            for b in range(2):
                g.memset(win[b][:, 0:16], 0.0).then_inc(pool_c, 1)
            g.memset(uT[:, :, 0:16], 0.0).then_inc(pool_c, 1)
            pool.wait_ge(pool_c, 9)
            n = 0
            for gr in range(NG):
                pool.wait_ge(u_c, gr // 2 + 1)
                src = uT[:, gr, :]
                for lev in range(gr + 1):
                    w = 1 << lev
                    if n >= 1:
                        pool.wait_ge(win_add, n)
                    if lev == 0 and gr >= 1:
                        pool.wait_ge(mix_ok, gr)
                    dst = win[lev % 2]
                    g.tensor_tensor(dst[:, 16:16 + S], src[:, 16:16 + S], src[:, 16 - w:16 - w + S],
                                    ALU.add).then_inc(win_add, 1)
                    n += 1
                    src = dst
            last = max(n for n in range(PER_BODY) if FIRST_PLACES[n] == RING)
            pool.wait_ge(chunks_used, -(-(last + 1) // PER_EXPERT) * PER_EXPERT)
            pool.dma_start(gain_f, final_norm_g.rearrange("(a d) -> a d", a=1).broadcast_to(
                [P, D])).then_inc(fg_in, 16)

        @block.scalar
        def _(act):
            a = nc.scalar
            for i, (src, lo, n) in enumerate(((norm1_g, 0, 8), (norm2_g, 8, 8), (sb_norm_g, 16, 4),
                                              (pool_scale, 20, 4))):
                v = src[0, :, :] if len(src.shape) == 3 else src.rearrange("l (r c) -> (l r) c", c=P)
                act.dma_start(vecs[lo:lo + n, :], v).then_inc(vecs_in[i], 16)
            act.wait_ge(edge_c, 3)
            a.activation(stat[:, 15:16], epsc[:], ACT.Sqrt).then_inc(warm, 1)
            for tt in range(TT):
                act.wait_ge(x_in[tt], 16)
                a.activation(xn[:, tt, :], xres[:, tt, :], ACT.Square,
                             accum_out=stat[:, tt:tt + 1]).then_inc(ssq, 1)
                act.wait_ge(ssq, tt + 1)
                a.activation(stat[:, 2 + tt:3 + tt], stat[:, tt:tt + 1], ACT.Sqrt, scale=1.0 / D,
                             bias=epsc[:]).then_inc(rtd, 1)
            act.wait_ge(vec_c, 1)
            for tt in range(TT):
                act.wait_ge(tr, 2 * tt + 2)
                for k in range(4):
                    a.activation(hT[:, 4 + k, tt * P:(tt + 1) * P],
                                 bank[5 + 2 * tt][:, k * P:(k + 1) * P], ACT.Copy,
                                 scale=G1[:, 4 + k:5 + k]).then_inc(tr_a, 1)

            act.dma_start(wpool[:], w_pool[0].rearrange("g c d -> c g d")).then_inc(wpool_in, 16)
            act.dma_start(wrouter[:], w_router[0].rearrange("(k p) e -> p k e", p=P)).then_inc(
                wrouter_in, 16)
            act.dma_start(brow[:], b_router.broadcast_to([P, NE])).then_inc(brow_in, 16)
            act.dma_start(wide[0:NE, :], b_down[0]).then_inc(bdown_in, 16)

            act.wait_ge(qk_ok, 1)
            for b in range(2):
                a.activation(qkT[:, 2 * b:2 * b + 2, :],
                             bank[b][:].rearrange("p (a t) -> p a t", a=2), ACT.Copy,
                             scale=float(HD) ** -0.5).then_inc(q_c, 1)

            def softplus_tail(j):
                t = lw[j % 2]
                act.wait_ge(z_ok, j + 1)
                if j >= 2:
                    act.wait_ge(zc_ok, j - 1)
                for h in range(2):
                    a.activation(t[:, h, :], bank[2 * (j % 2) + h][:, 0:384], ACT.Abs).then_inc(t1, 1)
                act.wait_ge(t1, 2 * j + 2)
                a.activation(t[:], t[:], ACT.Exp, scale=-1.0).then_inc(t2, 1)
                act.wait_ge(t2, j + 1)
                a.activation(t[:], t[:], ACT.Ln, bias=1.0).then_inc(t3, 1)

            def weights_exp(j):
                act.wait_ge(zc_ok, j + 1)
                if j >= 2:
                    act.wait_ge(o_ok, j - 1)
                for h in range(2):
                    a.activation(aw[j % 2][:, h, :], bank[2 * (j % 2) + h][:, 0:384],
                                 ACT.Exp).then_inc(a_exp, 1)

            def square_out(j):
                act.wait_ge(o_c, j + 1)
                if j >= 1:
                    act.wait_ge(ms_ok, j)
                a.activation(sq[:], mixT[j], ACT.Square).then_inc(sq_ok, 1)

            def pooled_out(b):
                act.wait_ge(pool_ok, b + 1)
                for g in (2 * b, 2 * b + 1):
                    a.activation(mixT[4 + g], bank[6 + b][:, (g % 2) * S:(g % 2 + 1) * S],
                                 ACT.Copy, scale=PSC[:, g:g + 1]).then_inc(poolT_ok, 1)

            def head_root(j):
                act.wait_ge(ms_ok, j + 1)
                lo = 0 if j >= 2 else S
                a.activation(head_rms(j), bank[4 + j % 2][:, lo:lo + S], ACT.Sqrt,
                             bias=epsc[:]).then_inc(hs_rt, 1)

            softplus_tail(0)
            softplus_tail(1)
            act.wait_ge(v_ok, 1)
            a.activation(vtok[:, 0, :], bank[4][:], ACT.Copy).then_inc(v_c, 1)
            weights_exp(0)
            weights_exp(1)
            square_out(0)
            softplus_tail(2)
            square_out(1)
            softplus_tail(3)
            head_root(0)
            head_root(1)
            pooled_out(0)
            weights_exp(2)
            weights_exp(3)
            square_out(2)
            pooled_out(1)
            square_out(3)
            head_root(2)
            head_root(3)
            for tt in range(TT):
                act.wait_ge(x2_ok, 2 * tt + 2)
                a.activation(xn[:, tt, :], xres[:, tt, :], ACT.Square,
                             accum_out=stat[:, 4 + tt:5 + tt]).then_inc(ssq, 1)
                act.wait_ge(ssq, tt + 3)
                a.activation(stat[:, 6 + tt:7 + tt], stat[:, 4 + tt:5 + tt], ACT.Sqrt,
                             scale=1.0 / D, bias=epsc[:]).then_inc(rtd, 1)
            act.wait_ge(tr, 8)
            a.activation(h2T[:, 4:8, P:2 * P], bank[7][:].rearrange("p (k t) -> p k t", k=4),
                         ACT.Copy).then_inc(tr_a, 1)
            for tt in range(TT):
                act.wait_ge(ntop, tt + 1)
                a.activation(ex[:, tt, :], lg[:, tt, 0:NE], ACT.Exp,
                             bias=negtop[:, tt:tt + 1]).then_inc(ex_ok, 1)

            act.wait_ge(flag_ok, 1)
            crowded = act.value_load(flag[0:1, 0:1], min_val=0, max_val=1)

            def fast_expert(e, r):
                act.wait_ge(gc_ok, e + 1)
                a.activation(sig, gatec, ACT.Sigmoid, scale=ALPHA).then_inc(sig_ok, 1)
                act.wait_ge(hT_ok, e + 1)
                a.activation(hidT, BG[:].rearrange("p (j t) -> p j t", j=4), ACT.Copy).then_inc(hT_c, 1)
                act.wait_ge(chunks_used, (e + 1) * PER_EXPERT)
                lo = (r % 2) * SLOTS
                a.activation(ypair[lo:lo + SLOTS, 0:HALF], BY[0:SLOTS, :], ACT.Copy).then_inc(y_lo, 1)

            with act.If(crowded):
                with act.Fori(0, NE) as e:
                    for tt in range(TT):
                        for hf in range(2):
                            n = e * 4 + (2 * tt + hf + 1)
                            act.wait_ge(n_gc, n)
                            a.activation(sig, gatec, ACT.Sigmoid, scale=ALPHA).then_inc(n_sig, 1)
                            act.wait_ge(n_hT, n)
                            a.activation(hidT_all[:, 4 * hf:4 * hf + 4, :],
                                         BG[:].rearrange("p (j t) -> p j t", j=4),
                                         ACT.Copy).then_inc(n_hTc, 1)
            with act.Else():
                with act.Fori(0, NE // 2) as q:
                    for r in range(2):
                        fast_expert(q * 2 + r, r)

            a.activation(stat[:, 15:16], epsc[:], ACT.Sqrt).then_inc(warm, 1)
            def squares(tt, hf):
                n = 2 * tt + hf
                act.wait_ge(sum_ok, n + 1)
                a.activation(xn[:, tt, hf * HALF:(hf + 1) * HALF],
                             xres[:, tt, hf * HALF:(hf + 1) * HALF], ACT.Square,
                             accum_out=stat[:, n:n + 1]).then_inc(fsq, 1)

            def final_root(tt):
                act.wait_ge(fadd, tt + 1)
                a.activation(stat[:, 10 + tt:11 + tt], stat[:, 8 + tt:9 + tt], ACT.Sqrt,
                             scale=1.0 / D, bias=epsc[:]).then_inc(frt, 1)

            squares(0, 0)
            squares(0, 1)
            squares(1, 0)
            final_root(0)
            squares(1, 1)
            final_root(1)

        @block.vector
        def _(dve):
            v = nc.vector
            v.memset(ones[:], 1.0).then_inc(ones_c, 1)
            v.memset(headmean[:], 0.0).then_inc(edge_c, 1)
            dve.wait_ge(edge_c, 1)
            for h in range(2):
                v.memset(headmean[h * HD:(h + 1) * HD, h * HD:(h + 1) * HD],
                         1.0 / HD).then_inc(consts, 1)
            v.memset(negones[:], -1.0).then_inc(edge_c, 1)
            v.memset(epsc[:], EPS).then_inc(edge_c, 1)
            v.memset(rank[:], -1.0).then_inc(edge_c, 1)
            v.memset(lg[:, :, NE:NE + 4], SENTINEL).then_inc(edge_c, 1)
            dve.wait_ge(iota_f, 1)
            for g in range(NG):
                v.tensor_scalar(edge[:, g, :], iota[:, 0:16], 1.0, float(WINDOWS[g]), ALU.add,
                                ALU.min).then_inc(edge_c, 1)
            dve.wait_ge(edge_c, 9)
            v.reciprocal(edge[:], edge[:]).then_inc(edge_c, 1)
            dve.wait_ge(edge_c, 10)
            for g in range(NG):
                v.tensor_scalar(edge[:, g, :], edge[:, g, :], float(WINDOWS[g]), None,
                                ALU.mult).then_inc(edge_c, 1)
            v.memset(gtab[:, :, :, 0:2], 0.0).then_inc(edge_c, 1)
            def normalise(tt, nth, col):
                dve.wait_ge(rtd, nth)
                v.reciprocal(stat[:, col:col + 1], stat[:, col:col + 1]).then_inc(rinv, 1)
                dve.wait_ge(rinv, nth)
                v.tensor_scalar(xn[:, tt, :], xres[:, tt, :], stat[:, col:col + 1], None,
                                ALU.mult).then_inc(xn_ok, 1)

            def gained(nth, tt, kh, dst, gains):
                dve.wait_ge(tr, nth)
                v.tensor_tensor(
                    dst[:, 4 * kh:4 * kh + 4, tt * P:(tt + 1) * P],
                    bank[4 + 2 * tt + kh][:].rearrange("p (k t) -> p k t", k=4),
                    gains[:, 4 * kh:4 * kh + 4].unsqueeze(2).to_broadcast([P, 4, P]),
                    ALU.mult).then_inc(tr_c, 1)

            for tt in range(TT):
                normalise(tt, tt + 1, 2 + tt)
            dve.wait_ge(vec_t, 1)
            v.tensor_copy(vecT[:], bank[0][:, 0:24]).then_inc(vec_c, 1)
            dve.wait_ge(vec_c, 1)
            for tt in range(TT):
                gained(2 * tt + 1, tt, 0, hT, G1)

            dve.wait_ge(qk_ok, 1)
            for b in range(2):
                v.tensor_copy(qkT[:, 4 + 2 * b:6 + 2 * b, :],
                              bank[2 + b][:].rearrange("p (a t) -> p a t", a=2)).then_inc(k_c, 1)

            def frames_out(b):
                dve.wait_ge(u_ok, b + 1)
                v.tensor_copy(uT[:, 2 * b:2 * b + 2, 16:16 + S],
                              bank[6 + b][:].rearrange("p (a t) -> p a t", a=2)).then_inc(u_c, 1)

            def softplus_head(j):
                t = lw[j % 2]
                dve.wait_ge(t3, j + 1)
                for h in range(2):
                    v.scalar_tensor_tensor(out=t[:, h, :], in0=bank[2 * (j % 2) + h][:, 0:384],
                                           scalar=0.0, in1=t[:, h, :], op0=ALU.max,
                                           op1=ALU.add).then_inc(l_add, 1)
                dve.wait_ge(l_add, 2 * j + 2)
                for c in (0, 256):
                    v.tensor_tensor(t[:, :, c:c + P], t[:, :, c:c + P],
                                    before[:].unsqueeze(1).to_broadcast([P, 2, P]),
                                    ALU.mult).then_inc(l_ok, 1)

            def weights_mask(j):
                t = aw[j % 2]
                dve.wait_ge(a_exp, 2 * j + 2)
                for c in (0, 256):
                    for h in range(2):
                        v.scalar_tensor_tensor(out=t[:, h, c:c + P], in0=t[:, h, c:c + P], scalar=1.0,
                                               in1=before[:], op0=ALU.min,
                                               op1=ALU.mult).then_inc(a_ok, 1)

            def heads_out(j):
                dve.wait_ge(o_ok, j + 1)
                v.tensor_copy(mixT[j], bank[4 + j % 2][:, 0:S]).then_inc(o_c, 1)

            def pool_mix(g):
                w = win[g % 2]
                dve.wait_ge(win_add, (g + 1) * (g + 2) // 2)
                v.tensor_tensor(w[:, 16:32], w[:, 16:32], edge[:, g, :], ALU.mult).then_inc(win_out, 1)
                dve.wait_ge(win_out, g + 1)
                v.scalar_tensor_tensor(out=uT[:, g, 16:16 + S], in0=w[:, 16:16 + S],
                                       scalar=1.0 / WINDOWS[g], in1=uT[:, g, 16:16 + S],
                                       op0=ALU.mult, op1=ALU.subtract).then_inc(mix_ok, 1)

            dve.wait_ge(wrouter_in, 16)
            v.tensor_tensor(wrouter[:], wrouter[:], G2.unsqueeze(2).to_broadcast([P, KD, NE]),
                            ALU.mult).then_inc(wrouter_c, 1)
            dve.wait_ge(consts, 8)
            v.tensor_copy(before_b[:], before[:]).then_inc(wrouter_c, 1)
            dve.wait_ge(edge_c, 15)
            softplus_head(0)
            softplus_head(1)
            dve.wait_ge(v_ok, 1)
            v.tensor_copy(vtok[:, 1, :], bank[5][:]).then_inc(v2_c, 1)
            weights_mask(0)
            weights_mask(1)
            frames_out(0)
            heads_out(0)
            heads_out(1)
            pool_mix(0)
            pool_mix(1)
            softplus_head(2)
            softplus_head(3)
            frames_out(1)
            weights_mask(2)
            weights_mask(3)
            pool_mix(2)
            heads_out(2)
            pool_mix(3)
            heads_out(3)
            for j in range(NPAIR):
                dve.wait_ge(hs_rt, j + 1)
                v.reciprocal(head_rms(j), head_rms(j)).then_inc(hs_inv, 1)
                dve.wait_ge(hs_inv, j + 1)
                v.scalar_tensor_tensor(out=mixT[j], in0=mixT[j], scalar=SBG[:, j:j + 1],
                                       in1=head_rms(j), op0=ALU.mult, op1=ALU.mult).then_inc(sbn, 1)
            def residual(tt, hf):
                dve.wait_ge(wo_ok, 1 if tt == 0 else 2 + hf)
                v.tensor_tensor(xres[:, tt, hf * HALF:(hf + 1) * HALF],
                                xres[:, tt, hf * HALF:(hf + 1) * HALF], bank[2 * tt + hf][:],
                                ALU.add).then_inc(x2_ok, 1)

            def moved(nth, tt, kh):
                dve.wait_ge(tr, nth)
                v.tensor_copy(h2T[:, 4 * kh:4 * kh + 4, tt * P:(tt + 1) * P],
                              bank[4 + 2 * tt + kh][:].rearrange("p (k t) -> p k t", k=4)
                              ).then_inc(tr_c, 1)

            residual(0, 0)
            residual(0, 1)
            moved(5, 0, 0)
            moved(6, 0, 1)
            normalise(0, 3, 6)
            residual(1, 0)
            residual(1, 1)
            moved(7, 1, 0)
            normalise(1, 4, 7)

            dve.wait_ge(brow_in, 16)
            for tt in range(TT):
                dve.wait_ge(lg_ok, tt + 1)
                v.scalar_tensor_tensor(out=lg[:, tt, 0:NE], in0=bank[tt][:, 0:NE],
                                       scalar=stat[:, 6 + tt:7 + tt], in1=brow[:], op0=ALU.mult,
                                       op1=ALU.add).then_inc(lg_c, 1)
                dve.wait_ge(lg_c, tt + 1)
                v.max(out=top8[:, tt, :], in_=lg[:, tt, 0:NE]).then_inc(mx, 1)
                dve.wait_ge(mx, tt + 1)
                v.memset(top8[:, tt, TOP_K:8], SENTINEL).then_inc(t8, 1)
                v.tensor_scalar(negtop[:, tt:tt + 1], top8[:, tt, 0:1], -1.0, None,
                                ALU.mult).then_inc(ntop, 1)
                dve.wait_ge(t8, tt + 1)
                v.match_replace(out=lgr[:, tt, :], in_to_replace=top8[:, tt, :],
                                in_values=lg[:, tt, :], imm_value=TAKEN).then_inc(mr, 1)
            dve.wait_ge(mr, 2)
            v.tensor_scalar(mask_b[:], lgr[:, :, 0:NE], TAKEN, None, ALU.is_ge).then_inc(maskb_ok, 1)
            v.tensor_scalar(mask[:], lgr[:, :, 0:NE], TAKEN, None, ALU.is_ge).then_inc(mask_ok, 1)

            def pick_rows(q, p):
                for tt in range(TT):
                    for r in range(2):
                        d = v.tensor_scalar(pick[p][:, tt, r * SLOTS:(r + 1) * SLOTS],
                                            iota[:, 1:SLOTS + 1], rank[:, tt, bass.ds(2 * q + r, 1)], None,
                                            ALU.is_equal)
                d.then_inc(pick_ok, 1)

            def scatter_matrix(q, p):
                dve.wait_ge(info_ok, q + 1)
                v.tensor_copy(info[:], BM[:, 0:3]).then_inc(info_c, 1)
                dve.wait_ge(info_c, q + 1)
                for r in range(2):
                    lo = r * SLOTS
                    d = v.tensor_scalar(scat[p][lo:lo + SLOTS, :], iota[lo:lo + SLOTS, :],
                                        info[lo:lo + SLOTS, 2:3], info[lo:lo + SLOTS, r:r + 1],
                                        ALU.is_equal, ALU.mult)
                d.then_inc(scat_ok, 1)

            def gathered(q, p, kh, ready, done, src=BM):
                dve.wait_ge(ready, q + 1)
                v.tensor_tensor(xT[p][:, 4 * kh:4 * kh + 4, :],
                                src[:].rearrange("p (k t) -> p k t", k=4),
                                G2[:, 4 * kh:4 * kh + 4].unsqueeze(2).to_broadcast([P, 4, P]),
                                ALU.mult).then_inc(done, 1)

            dve.wait_ge(rank_ok, 1)
            dve.wait_ge(mask_ok, 1)
            v.scalar_tensor_tensor(out=rank[:, :, 0:NE],
                                   in0=bank[2][:, 0:TT * NE].rearrange("p (a e) -> p a e", a=TT),
                                   scalar=1.0, in1=mask[:], op0=ALU.add,
                                   op1=ALU.mult).then_inc(rank_c, 1)
            v.reduce_max(most[:, 0:1], bank[2][0:1, TT * NE:(TT + 1) * NE], AX_X).then_inc(cnt_m, 1)
            dve.wait_ge(rank_c, 1)
            pick_rows(0, 0)
            dve.wait_ge(cnt_m, 1)
            v.tensor_scalar(flag[:], most[:, 0:1], float(SLOTS), None, ALU.is_gt).then_inc(flag_ok, 1)
            dve.wait_ge(ex_ok, 2)
            v.tensor_tensor(exm[:], ex[:], mask[:], ALU.mult).then_inc(exm_ok, 1)
            dve.wait_ge(exm_ok, 1)
            v.reduce_sum(stat[:, 12:14], exm[:], AX_X).then_inc(den, 1)
            dve.wait_ge(den, 1)
            dve.wait_ge(warm, 1)
            v.reciprocal(stat[:, 14:16], stat[:, 12:14]).then_inc(den, 1)
            dve.wait_ge(den, 2)
            for tt in range(TT):
                v.tensor_scalar(gate[:, tt, :], exm[:, tt, :], stat[:, 14 + tt:15 + tt], None,
                                ALU.mult).then_inc(gate_ok, 1)
            dve.wait_ge(gate_ok, 2)
            dve.wait_ge(pool_c, 6)
            for tt in range(TT):
                v.tensor_copy(gtab[:, tt, 0:NE // 2, 0:2],
                              gate[:, tt, :].rearrange("p (q r) -> p q r", r=2)).then_inc(gtab_ok, 1)
            gathered(0, 0, 0, ga_ok, xa_ok)
            dve.wait_ge(gT_ok, 1)
            v.tensor_copy(gateT[:], bank[3][0:NE, 0:S]).then_inc(gT_c, 1)

            dve.wait_ge(flag_ok, 1)
            crowded = dve.value_load(flag[0:1, 0:1], min_val=0, max_val=1)

            def swiglu(n, ready, gbank, ubank, gc, uc, sg, tm, hh, before_up=None):
                dve.wait_ge(ready[0], ready[1])
                v.tensor_scalar(gatec, gbank[:], LIMIT, None, ALU.min).then_inc(gc, 1)
                if before_up is not None:
                    dve.wait_ge(before_up[0], before_up[1])
                v.tensor_scalar(upc, ubank[:], LIMIT, -LIMIT, ALU.min, ALU.max).then_inc(uc, 1)
                dve.wait_ge(gc, n)
                dve.wait_ge(uc, n)
                v.scalar_tensor_tensor(out=upc, in0=upc, scalar=1.0, in1=gatec, op0=ALU.add,
                                       op1=ALU.mult).then_inc(tm, 1)
                dve.wait_ge(tm, n)
                dve.wait_ge(sg, n)
                v.tensor_tensor(upc, upc, sig, ALU.mult).then_inc(hh, 1)

            def rows_out(e, r):
                dve.wait_ge(chunks_used, (e + 1) * PER_EXPERT)
                lo = (r % 2) * SLOTS
                v.tensor_copy(ypair[lo:lo + SLOTS, HALF:D], BY[SLOTS:P, :]).then_inc(y_hi, 1)

            def fast_pair(q, p):
                pick_rows(q + 1, 1 - p)
                swiglu(2 * q + 1, (chunks_used, q * (2 * PER_EXPERT) + UP_CHUNKS), BG, BU, gc_ok, uc_ok, sig_ok, t_ok, h_ok)
                scatter_matrix(q + 1, 1 - p)
                rows_out(2 * q, 0)
                swiglu(2 * q + 2, (chunks_used, q * (2 * PER_EXPERT) + (PER_EXPERT + UP_CHUNKS)), BG, BU, gc_ok, uc_ok, sig_ok, t_ok, h_ok)
                gathered(q + 1, 1 - p, 0, ga_ok, xa_ok)
                gathered(q + 1, 1 - p, 1, gb_ok, xb_ok)
                rows_out(2 * q + 1, 1)

            with dve.If(crowded):
                for tt in range(TT):
                    for kh in range(2):
                        gained(9 + 2 * tt + kh, tt, kh, h2T, G2)
                dve.wait_ge(bd_ok, 1)
                for tt in range(TT):
                    for hf in range(2):
                        v.tensor_copy(xn[:, tt, hf * HALF:(hf + 1) * HALF],
                                      bank[2 * tt + hf][:]).then_inc(n_acc, 1)
                with dve.Fori(0, NE) as e:
                    for tt in range(TT):
                        for hf in range(2):
                            swiglu(e * 4 + (2 * tt + hf + 1), (n_up, e * 2 + (tt + 1)), bank[hf],
                                   bank[2 + hf], n_gc, n_uc, n_sig, n_t, n_h,
                                   (n_sig, e * 4 + (2 * tt + hf + 1)))
                        if tt == 0:
                            dve.wait_ge(n_y, e + 1)
                        else:
                            dve.wait_ge(chunks_used, (e + 1) * PER_EXPERT)
                        dve.wait_ge(n_acc, e * 4 + (2 * tt + 4))
                        for hf in range(2):
                            v.scalar_tensor_tensor(
                                out=xn[:, tt, hf * HALF:(hf + 1) * HALF], in0=bank[5 + hf][:],
                                scalar=gate[:, tt, bass.ds(e, 1)],
                                in1=xn[:, tt, hf * HALF:(hf + 1) * HALF], op0=ALU.mult,
                                op1=ALU.add).then_inc(n_acc, 1)
                dve.wait_ge(n_acc, 4 * NE + 4)
                for tt in range(TT):
                    for hf in range(2):
                        v.tensor_tensor(xres[:, tt, hf * HALF:(hf + 1) * HALF],
                                        xres[:, tt, hf * HALF:(hf + 1) * HALF],
                                        xn[:, tt, hf * HALF:(hf + 1) * HALF],
                                        ALU.add).then_inc(sum_ok, 1)
            with dve.Else():
                gathered(0, 0, 1, gb_ok, xb_ok, BY)
                scatter_matrix(0, 0)
                with dve.Fori(0, NE // BODY) as i:
                    for p in range(2):
                        fast_pair(i * 2 + p, p)
                for tt in range(TT):
                    for hf in range(2):
                        dve.wait_ge(last_ok, 2 * tt + hf + 1)
                        v.tensor_tensor(xres[:, tt, hf * HALF:(hf + 1) * HALF],
                                        xres[:, tt, hf * HALF:(hf + 1) * HALF],
                                        bank[2 * tt + hf][:], ALU.add).then_inc(sum_ok, 1)

            def sum_squares(tt):
                dve.wait_ge(fsq, 2 * tt + 2)
                v.tensor_tensor(stat[:, 8 + tt:9 + tt], stat[:, 2 * tt:2 * tt + 1],
                                stat[:, 2 * tt + 1:2 * tt + 2], ALU.add).then_inc(fadd, 1)

            def final_inverse(tt):
                dve.wait_ge(frt, tt + 1)
                v.reciprocal(stat[:, 10 + tt:11 + tt], stat[:, 10 + tt:11 + tt]).then_inc(finv, 1)
                dve.wait_ge(finv, tt + 1)

            def rows_final(tt, hf):
                v.scalar_tensor_tensor(out=xn[:, tt, hf * HALF:(hf + 1) * HALF],
                                       in0=xres[:, tt, hf * HALF:(hf + 1) * HALF],
                                       scalar=stat[:, 10 + tt:11 + tt],
                                       in1=gain_f[:, hf * HALF:(hf + 1) * HALF], op0=ALU.mult,
                                       op1=ALU.mult).then_inc(fin, 1)

            dve.wait_ge(fg_in, 16)
            sum_squares(0)
            final_inverse(0)
            rows_final(0, 0)
            sum_squares(1)
            rows_final(0, 1)
            final_inverse(1)
            rows_final(1, 0)
            rows_final(1, 1)

        @block.tensor
        def _(pe):
            t = nc.tensor

            def mm(o, l, r, start=False, stop=False):
                return t.matmul(o, l, r, start=start, stop=stop, skip_group_check=True)

            def keep_warm(n):
                for _ in range(n):
                    mm(bank[3][:], ones[:], ones[:].unsqueeze(1).to_broadcast([P, 4, P]), start=True)

            pe.wait_ge(ones_c, 1)
            keep_warm(20)
            for i in range(4):
                pe.wait_ge(vecs_in[i], 16)
            pe.wait_ge(consts, 8)
            t.transpose(bank[0][:, 0:24], vecs[:], ident[0:24, 0:24]).then_inc(vec_t, 1)

            def turn(src, tt, halves=(0, 1)):
                for kh in halves:
                    for k in range(4):
                        lo = (4 * kh + k) * P
                        m = t.transpose(bank[4 + 2 * tt + kh][:, k * P:(k + 1) * P],
                                        src[:, tt, lo:lo + P], ident[:])
                    m.then_inc(tr, 1)

            for tt in range(TT):
                pe.wait_ge(xn_ok, tt + 1)
                turn(xn, tt)
            pe.wait_ge(tr_c, 2)
            for k in range(KD):
                if k == 4:
                    pe.wait_ge(tr_a, 8)
                pe.wait_ge(wqk_in[k], 16)
                for c in range(8):
                    m = mm(bank[c // 2][:, (c % 2) * S:(c % 2 + 1) * S],
                           w_qk[:, k, c * P:(c + 1) * P], hT[:, k, :],
                           start=(k == 0 and c % 2 == 0), stop=(k == KD - 1 and c % 2 == 1))
            m.then_inc(qk_ok, 1)

            def project_v(steps):
                for k in steps:
                    if k % 4 == 0:
                        pe.wait_ge(wv_in[k // 4], 16)
                    for tt in range(TT):
                        m = mm(bank[4 + tt][:], hT[:, k, tt * P:(tt + 1) * P], w_v[:, k, :],
                               start=(k == 0), stop=(k == KD - 1))
                if k == KD - 1:
                    m.then_inc(v_ok, 1)

            def project_u(b):
                for k in range(KD):
                    if b == 0 and k % 4 == 0:
                        pe.wait_ge(wu_in[k // 4], 16)
                    for c in (2 * b, 2 * b + 1):
                        m = mm(bank[6 + b][:, (c % 2) * S:(c % 2 + 1) * S],
                               w_u[:, k, c * P:(c + 1) * P], hT[:, k, :],
                               start=(k == 0 and c % 2 == 0), stop=(k == KD - 1 and c % 2 == 1))
                m.then_inc(u_ok, 1)

            def scores(j):
                if j >= 2:
                    pe.wait_ge(a_exp, 2 * j - 2)
                for h in range(2):
                    zb = bank[2 * (j % 2) + h]
                    q = qkT[h * HD:(h + 1) * HD, j, :]
                    kk = qkT[h * HD:(h + 1) * HD, NPAIR + j, :]
                    mm(zb[:, 0:S], kk[:, 0:P], q, start=True)
                    m = mm(zb[:, S:S + P], kk[:, P:S], q[:, P:S])
                m.then_inc(z_ok, 1)

            def after_sums(j):
                pe.wait_ge(l_ok, 2 * j + 2)
                for h in range(2):
                    zb = bank[2 * (j % 2) + h]
                    lt = lw[j % 2][:, h, :]
                    mm(zb[:, 0:S], negtri[:], lt[:, 0:S])
                    mm(zb[:, P:S], negones[:], lt[:, S:S + P])
                    m = mm(zb[:, S:S + P], negtri[:], lt[:, S:S + P], stop=True)
                m.then_inc(zc_ok, 1)

            def values(j):
                pe.wait_ge(a_ok, 4 * j + 4)
                if j >= 2:
                    pe.wait_ge(o_c, j - 1)
                for h in range(2):
                    hd = (2 * j + h) * HD
                    ob = bank[4 + j % 2][h * HD:(h + 1) * HD, :]
                    wt = aw[j % 2][:, h, :]
                    mm(ob[:, 0:S], vtok[:, 0, hd:hd + HD], wt[:, 0:S], start=True)
                    m = mm(ob[:, P:S], vtok[:, 1, hd:hd + HD], wt[:, S:S + P], stop=True)
                m.then_inc(o_ok, 1)

            def mean_squares(j):
                pe.wait_ge(sq_ok, j + 1)
                lo = 0 if j >= 2 else S
                mm(bank[4 + j % 2][:, lo:lo + S], headmean[:], sq[:], start=True,
                   stop=True).then_inc(ms_ok, 1)

            def map_pooled(b):
                if b == 0:
                    pe.wait_ge(wpool_in, 16)
                for g in (2 * b, 2 * b + 1):
                    pe.wait_ge(mix_ok, g + 1)
                    m = mm(bank[6 + b][:, (g % 2) * S:(g % 2 + 1) * S], wpool[:, g, :],
                           uT[:, g, 16:16 + S], start=(g % 2 == 0), stop=(g % 2 == 1))
                m.then_inc(pool_ok, 1)

            def output(tt, n, halves=(0, 1)):
                k = WO_ROWS[n // 2] + n % 2
                if n % 2 == 0:
                    pe.wait_ge(wout_in[n // 2], 16)
                if k >= 4:
                    pe.wait_ge(poolT_ok, k - 3)
                else:
                    pe.wait_ge(sbn, k + 1)
                for hf in halves:
                    m = mm(bank[2 * tt + hf][:], mixT[k][:, tt * P:(tt + 1) * P],
                           w_o[:, n, hf * HALF:(hf + 1) * HALF], start=(n == 0),
                           stop=(n == KD - 1))
                return m

            pe.wait_ge(edge_c, 15)
            project_v(range(0, 1))
            pe.wait_ge(q_c, 2)
            pe.wait_ge(k_c, 2)
            scores(0)
            scores(1)
            project_v(range(1, KD))
            after_sums(0)
            after_sums(1)
            project_u(0)
            pe.wait_ge(v_c, 1)
            pe.wait_ge(v2_c, 1)
            values(0)
            values(1)
            scores(2)
            scores(3)
            mean_squares(0)
            project_u(1)
            mean_squares(1)
            map_pooled(0)
            after_sums(2)
            after_sums(3)
            values(2)
            output(0, 0)
            output(0, 1)
            values(3)
            map_pooled(1)
            mean_squares(2)
            output(0, 2)
            output(0, 3)
            mean_squares(3)
            for n in range(4):
                m = output(1, n)
            m.then_inc(wo_half, 1)
            for n in range(4, KD):
                m = output(0, n)
            m.then_inc(wo_ok, 1)
            output(1, 4)
            output(1, 5)

            def logits(tt):
                for k in range(KD):
                    if tt == 0 and k % 4 == 0:
                        pe.wait_ge(tr_c, 3 + k // 4)
                    elif k == 0:
                        pe.wait_ge(tr_c, 5)
                    elif k == 4:
                        pe.wait_ge(tr_a, 9)
                    m = mm(bank[tt][:, 0:4 * NE], h2T[:, k, tt * P:(tt + 1) * P],
                           wrouter[:, k, :].unsqueeze(1).to_broadcast([P, 4, NE]),
                           start=(k == 0), stop=(k == KD - 1))
                m.then_inc(lg_ok, 1)

            pe.wait_ge(x2_ok, 1)
            turn(xres, 0, (0,))
            pe.wait_ge(x2_ok, 2)
            turn(xres, 0, (1,))
            output(1, 6, (0,))
            output(1, 7, (0,)).then_inc(wo_ok, 1)
            pe.wait_ge(wrouter_c, 2)
            logits(0)
            output(1, 6, (1,))
            output(1, 7, (1,)).then_inc(wo_ok, 1)
            pe.wait_ge(x2_ok, 3)
            turn(xres, 1, (0,))
            pe.wait_ge(x2_ok, 4)
            turn(xres, 1, (1,))
            logits(1)
            pe.wait_ge(bias_in[0], 16)
            mm(BG[:], bsel[:, 0, :], bias[:, 0, :], start=True)
            keep_warm(1)
            pe.wait_ge(maskb_ok, 1)
            mm(bank[2][:, 0:2 * NE], before_b[:], mask_b[:].rearrange("p a e -> p (a e)"), start=True)
            mm(bank[2][:, NE:2 * NE], ones[:], mask_b[:, 0, :])
            mm(bank[2][:, 2 * NE:3 * NE], ones[:], mask_b[:, 0, :])
            mm(bank[2][:, 2 * NE:3 * NE], ones[:], mask_b[:, 1, :], stop=True).then_inc(rank_ok, 1)

            def slot_info(q, p):
                for tt in range(TT):
                    m = mm(BM[:, 0:3], pick[p][:, tt, :], gtab[:, tt, bass.ds(q, 1), :].rearrange(
                        "p a b -> p (a b)"), start=(tt == 0), stop=(tt == 1))
                m.then_inc(info_ok, 1)

            def gather(q, p, kh, free, done, dst=BM):
                if free is not None:
                    pe.wait_ge(free, q + 1)
                for k in range(4):
                    f = (4 * kh + k) * P
                    for tt in range(TT):
                        m = mm(dst[:, k * P:(k + 1) * P], xn[:, tt, f:f + P], pick[p][:, tt, :],
                               start=(k == 0 and tt == 0), stop=(k == 3 and tt == 1))
                m.then_inc(done, 1)

            mm(BU[:], bsel[:, 1, :], bias[:, 0, :], start=True)
            keep_warm(1)
            pe.wait_ge(pick_ok, 1)
            pe.wait_ge(xn_ok, 4)
            gather(0, 0, 0, None, ga_ok)
            pe.wait_ge(gate_ok, 2)
            for tt in range(TT):
                m = t.transpose(bank[3][0:NE, tt * P:(tt + 1) * P], gate[:, tt, :], ident[:])
            m.then_inc(gT_ok, 1)

            def add_b_down():
                pe.wait_ge(bdown_in, 16)
                pe.wait_ge(gT_c, 1)
                for tt in range(TT):
                    for hf in range(2):
                        m = mm(bank[2 * tt + hf][:], gateT[:, tt * P:(tt + 1) * P],
                               wide[0:NE, hf * HALF:(hf + 1) * HALF], start=True)
                m.then_inc(bd_ok, 1)

            pe.wait_ge(flag_ok, 1)
            crowded = pe.value_load(flag[0:1, 0:1], min_val=0, max_val=1)

            def chunk_wait(i, m, first):
                slot = slot_of(m, first)
                if first:
                    pe.wait_ge(chunk_in[slot], 16 * loads_of(m, True))
                else:
                    between = 16 * (PER_BODY // RING)
                    pe.wait_ge(chunk_in[slot], i * between + (16 * loads_of(m, False) - between))
                return slot

            def combine(q, p):
                pe.wait_ge(scat_ok, q + 1)
                pe.wait_ge(y_lo, 2 * q + 2)
                pe.wait_ge(y_hi, 2 * q + 2)
                for tt in range(TT):
                    for hf in range(2):
                        m = mm(bank[2 * tt + hf][:], scat[p][:, tt * P:(tt + 1) * P],
                               ypair[:, hf * HALF:(hf + 1) * HALF])
                m.then_inc(comb_ok, 1)

            def fast_expert(i, r, q, p, body0, not_first):
                e = 2 * q + r % 2
                m0 = r * PER_EXPERT
                cols = slice((r % 2) * SLOTS, (r % 2 + 1) * SLOTS)
                first = not not_first and r == 0
                if not first:
                    pe.wait_ge(bias_in[r % 2], i * 32 + 16 * (r // 2 + 1))
                    mm(BG[:], bsel[:, 0, :], bias[:, r % 2, :], start=True)
                    mm(BU[:], bsel[:, 1, :], bias[:, r % 2, :], start=True).then_inc(bias_used, 1)
                    if r % 2 == 0:
                        pe.wait_ge(xb_ok, q + 1)
                else:
                    pe.wait_ge(xa_ok, 1)
                for k in range(KD):
                    if first and k == 4:
                        gather(0, 0, 1, None, gb_ok, BY)
                        pe.wait_ge(gtab_ok, 2)
                        slot_info(0, 0)
                        pe.wait_ge(xb_ok, 1)
                    slot = chunk_wait(i, m0 + k, body0)
                    for gu, b in ((0, BG), (1, BU)):
                        for hf in range(2):
                            m = mm(b[hf * SLOTS:(hf + 1) * SLOTS, :], xT[p][:, k, cols],
                                   up_w(slot, gu, hf), stop=(k == KD - 1))
                            if first and k == 0 and gu == 0 and hf == 0:
                                m.then_inc(bias_used, 1)
                    m.then_inc(chunks_used, 1)
                if r % 2 == 0:
                    if not_first:
                        combine(q - 1, 1 - p)
                    else:
                        add_b_down()
                else:
                    gather(q + 1, 1 - p, 0, info_c, ga_ok)
                pe.wait_ge(h_ok, e + 1)
                for j in range(4):
                    m = t.transpose(BG[:, j * P:(j + 1) * P], upc[:, j * P:(j + 1) * P], ident[:])
                m.then_inc(hT_ok, 1)
                if r % 2 == 0:
                    pe.wait_ge(pick_ok, q + 2)
                    slot_info(q + 1, 1 - p)
                else:
                    gather(q + 1, 1 - p, 1, xa_ok, gb_ok)
                pe.wait_ge(hT_c, e + 1)
                for c in range(DOWN_CHUNKS):
                    n = m0 + UP_CHUNKS + c
                    slot = chunk_wait(i, n, body0)
                    for s in range(2):
                        f = 2 * c + s
                        half, j = f // 4, f % 4
                        for hf in range(2):
                            m = mm(BY[hf * SLOTS:(hf + 1) * SLOTS, :],
                                   hidT[:, j, half * SLOTS:(half + 1) * SLOTS], down_w(slot, s, hf),
                                   start=(f == 0), stop=(f == KF - 1))
                    m.then_inc(chunks_used, 1)

            def fast_body(i, first):
                for r in range(BODY):
                    q = i * 2 + r // 2
                    fast_expert(i, r, q, r // 2, first, not (first and r < 2))

            with pe.If(crowded):
                add_b_down()
                pe.wait_ge(xa_ok, 1)
                for tt in range(TT):
                    turn(xn, tt)
                pe.wait_ge(n_acc, 4)
                pe.wait_ge(tr_c, 9)

                def all_tokens(i, r, first):
                    e = i * BODY + r
                    m0 = r * PER_EXPERT
                    pe.wait_ge(bias_in[r % 2], i * 32 + 16 * (r // 2 + 1))
                    for tt in range(TT):
                        for b in range(4):
                            m = mm(bank[b][:], bsel[:, 2 + b, :], bias[:, r % 2, :], start=True)
                        if tt == TT - 1:
                            m.then_inc(bias_used, 1)
                        for k in range(KD):
                            slot = slot_of(m0 + k, first)
                            if tt == 0:
                                chunk_wait(i, m0 + k, first)
                            for b in range(4):
                                m = mm(bank[b][:], h2T[:, k, tt * P:(tt + 1) * P],
                                       up_w(slot, b // 2, b % 2), stop=(k == KD - 1))
                        m.then_inc(n_up, 1)
                        for hf in range(2):
                            n = e * 4 + (2 * tt + hf + 1)
                            pe.wait_ge(n_h, n)
                            if hf == 1:
                                pe.wait_ge(n_hTc, e * 4 + (2 * tt + 1))
                            for j in range(4):
                                m = t.transpose(BG[:, j * P:(j + 1) * P],
                                                upc[:, j * P:(j + 1) * P], ident[:])
                            m.then_inc(n_hT, 1)
                        pe.wait_ge(n_hTc, e * 4 + (2 * tt + 2))
                        pe.wait_ge(n_acc, e * 4 + (2 * tt + 4))
                        for f in range(KF):
                            n = m0 + UP_CHUNKS + f // 2
                            slot = slot_of(n, first)
                            if tt == 0 and f % 2 == 0:
                                chunk_wait(i, n, first)
                            for hf in range(2):
                                m = mm(bank[5 + hf][:], hidT_all[:, f, :], down_w(slot, f % 2, hf),
                                       start=(f == 0), stop=(f == KF - 1))
                        if tt == 0:
                            m.then_inc(n_y, 1)
                        else:
                            m.then_inc(chunks_used, PER_EXPERT)

                for r in range(BODY):
                    all_tokens(0, r, True)
                with pe.Fori(1, NBODY) as i:
                    for r in range(BODY):
                        all_tokens(i, r, False)
            with pe.Else():
                fast_body(0, True)
                with pe.Fori(1, NBODY) as i:
                    fast_body(i, False)
                pe.wait_ge(scat_ok, NE // 2)
                pe.wait_ge(y_lo, NE)
                pe.wait_ge(y_hi, NE)
                for tt in range(TT):
                    for hf in range(2):
                        mm(bank[2 * tt + hf][:], scat[1][:, tt * P:(tt + 1) * P],
                           ypair[:, hf * HALF:(hf + 1) * HALF], stop=True).then_inc(last_ok, 1)


_INS = ["x", "norm1_g", "w_in", "sb_norm_g", "w_pool", "pool_scale", "w_out", "norm2_g", "w_router",
        "b_router", "w_gate_up", "b_gate_up", "w_down", "b_down", "final_norm_g"]


def kernel(**inputs):
    import numpy as _np
    import concourse.bacc as _bacc
    from concourse import mybir as _mybir
    from concourse.bass_utils import run_bass_kernel_spmd as _run

    nc = _bacc.Bacc("TRN2", target_bir_lowering=False, num_devices=1)
    arrays, args = {}, []
    for name in _INS:
        a = _np.ascontiguousarray(inputs[name])
        arrays[f"in_{name}_dram"] = a
        args.append(nc.dram_tensor(f"in_{name}_dram", a.shape, _mybir.dt.from_np(a.dtype),
                                   kind="ExternalInput").ap())
    shape = tuple(inputs["x"].shape)
    args.append(nc.dram_tensor("out_0_dram", shape, _mybir.dt.float32, kind="ExternalOutput").ap())
    build(nc, *args)
    r = _run(nc, [arrays], core_ids=[0])
    return r.results[0]["out_0_dram"]
```
